# Optimizing a Trainium2 kernel written in Bass

```python
import jax, jax.numpy as jnp
from jax import lax
import numpy as np

D_MODEL = 1024
BATCH = 1
SEQ = 512
DEPTH = 2
DEC_BATCH = 8
DEC_SEQ = 4
PAST_LEN = 2048
PAGE_SIZE = 128

HEAD_DIM = 64
N_Q_HEADS = 12
N_KV_HEADS = 4
GQA_GROUP = N_Q_HEADS // N_KV_HEADS
WINDOW = 128
Q_BLOCK = WINDOW
ROPE_THETA = 10000.0
CONV_CH = N_Q_HEADS * HEAD_DIM
CONV_W = 3
N_MEM = 256
N_X_HEADS = 4
X_DIM = N_X_HEADS * HEAD_DIM
D_FF = 4 * D_MODEL
N_MIXERS = 2
N_ATT_LAYERS = (DEPTH + 1) // 2
N_CONV_LAYERS = DEPTH // 2
ATT_IN = N_Q_HEADS * HEAD_DIM + 2 * N_KV_HEADS * HEAD_DIM + X_DIM
CONV_IN = 3 * CONV_CH + X_DIM
MIX_OUT = CONV_CH + X_DIM
EPS = 1e-6
NEG = -1e30

kernel_name = "hybrid_swa_sink_shortconv_memxattn_step"

def _rms_norm(x, g):
    xf = x.astype(jnp.float32)
    y = xf * lax.rsqrt(jnp.mean(xf * xf, axis=-1, keepdims=True) + EPS) * g.astype(jnp.float32)
    return y.astype(x.dtype)

def _rope(x, pos):
    half = HEAD_DIM // 2
    inv = ROPE_THETA ** (-jnp.arange(half, dtype=jnp.float32) * 2.0 / HEAD_DIM)
    ang = pos[:, None] * inv[None, :]
    cos = jnp.cos(ang)[:, None, :]
    sin = jnp.sin(ang)[:, None, :]
    xf = x.astype(jnp.float32)
    x1, x2 = xf[..., :half], xf[..., half:]
    return jnp.concatenate([x1 * cos - x2 * sin, x2 * cos + x1 * sin], axis=-1).astype(x.dtype)

def _sink_softmax(s, mask, sink):
    s = jnp.where(mask, s, NEG)
    sink = sink.astype(jnp.float32)
    m = jnp.maximum(jnp.max(s, axis=-1, keepdims=True), sink)
    p = jnp.exp(s - m)
    return p / (jnp.sum(p, axis=-1, keepdims=True) + jnp.exp(sink - m))

def _swa_prompt(q, k, v, sink):
    n, t = q.shape[0], q.shape[1]
    nb = t // Q_BLOCK
    qb = q.reshape(n, nb, Q_BLOCK, N_KV_HEADS, GQA_GROUP, HEAD_DIM)
    pad = jnp.zeros((n, Q_BLOCK, N_KV_HEADS, HEAD_DIM), k.dtype)
    kb = jnp.concatenate([pad, k], axis=1).reshape(n, nb + 1, Q_BLOCK, N_KV_HEADS, HEAD_DIM)
    vb = jnp.concatenate([pad.astype(v.dtype), v], axis=1).reshape(n, nb + 1, Q_BLOCK, N_KV_HEADS, HEAD_DIM)
    kb = jnp.concatenate([kb[:, :-1], kb[:, 1:]], axis=2)
    vb = jnp.concatenate([vb[:, :-1], vb[:, 1:]], axis=2)
    s = jnp.einsum("bnqkgd,bnskd->bnkgqs", qb, kb, preferred_element_type=jnp.float32) * (HEAD_DIM ** -0.5)
    blk = jnp.arange(nb)[:, None, None] * Q_BLOCK
    qpos = blk + jnp.arange(Q_BLOCK)[None, :, None]
    kpos = blk - Q_BLOCK + jnp.arange(2 * Q_BLOCK)[None, None, :]
    d = qpos - kpos
    mask = (d >= 0) & (d < WINDOW) & (kpos >= 0)
    mask = mask[None, :, None, None]
    pr = _sink_softmax(s, mask, sink.reshape(N_KV_HEADS, GQA_GROUP, 1, 1))
    o = jnp.einsum("bnkgqs,bnskd->bnqkgd", pr.astype(vb.dtype), vb)
    return o.reshape(n, t, N_Q_HEADS, HEAD_DIM)

def _swa_sample(q, k, v, kbuf, vbuf, sink):
    n, t = q.shape[0], q.shape[1]
    nbuf = kbuf.shape[1]
    kk = jnp.concatenate([kbuf.astype(k.dtype), k], axis=1)
    vv = jnp.concatenate([vbuf.astype(v.dtype), v], axis=1)
    qg = q.reshape(n, t, N_KV_HEADS, GQA_GROUP, HEAD_DIM)
    s = jnp.einsum("bqkgd,bskd->bkgqs", qg, kk, preferred_element_type=jnp.float32) * (HEAD_DIM ** -0.5)
    qpos = PAST_LEN + jnp.arange(t)
    kpos = PAST_LEN - nbuf + jnp.arange(nbuf + t)
    d = qpos[:, None] - kpos[None, :]
    mask = (d >= 0) & (d < WINDOW)
    pr = _sink_softmax(s, mask, sink.reshape(N_KV_HEADS, GQA_GROUP, 1, 1))
    o = jnp.einsum("bkgqs,bskd->bqkgd", pr.astype(vv.dtype), vv).reshape(n, t, N_Q_HEADS, HEAD_DIM)
    return o, kk[:, -WINDOW:], vv[:, -WINDOW:]

def _causal_conv(u, prefix, w):
    t = u.shape[1]
    full = jnp.concatenate([prefix.astype(u.dtype), u], axis=1)
    y = full[:, 0:t] * w[0]
    for j in range(1, CONV_W):
        y = y + full[:, j:j + t] * w[j]
    return y, full[:, -(CONV_W - 1):]

def _mem_kv(mem, g, w_kv, k_g):
    n = mem.shape[0]
    kv = _rms_norm(mem, g) @ w_kv
    mk = kv[..., :X_DIM].reshape(n, N_MEM, N_X_HEADS, HEAD_DIM)
    mv = kv[..., X_DIM:].reshape(n, N_MEM, N_X_HEADS, HEAD_DIM)
    return _rms_norm(mk, k_g), mv

def _cross_attend(q, mk, mv):
    s = jnp.einsum("bthd,bmhd->bhtm", q, mk.astype(q.dtype), preferred_element_type=jnp.float32) * (HEAD_DIM ** -0.5)
    p = jax.nn.softmax(s, axis=-1)
    return jnp.einsum("bhtm,bmhd->bthd", p.astype(mv.dtype), mv)

def _trunk(x, pos0, mem_k, mem_v, swa_k_in, swa_v_in, conv_in, is_prompt, p):
    n, t = x.shape[0], x.shape[1]
    pos = pos0 + jnp.arange(t, dtype=jnp.float32)
    new_k, new_v, new_conv = [], [], []
    for i in range(DEPTH):
        j = i // N_MIXERS
        h = _rms_norm(x, p["norm_mix"][i])
        if i % N_MIXERS == 0:
            z = h @ p["w_in_att"][j]
            c0 = N_Q_HEADS * HEAD_DIM
            c1 = c0 + N_KV_HEADS * HEAD_DIM
            c2 = c1 + N_KV_HEADS * HEAD_DIM
            q = z[..., :c0].reshape(n, t, N_Q_HEADS, HEAD_DIM)
            k = z[..., c0:c1].reshape(n, t, N_KV_HEADS, HEAD_DIM)
            v = z[..., c1:c2].reshape(n, t, N_KV_HEADS, HEAD_DIM)
            qx = z[..., c2:]
            q = _rope(_rms_norm(q, p["q_norm_att"][j]), pos)
            k = _rope(_rms_norm(k, p["k_norm_att"][j]), pos)
            if is_prompt:
                o_self = _swa_prompt(q, k, v, p["sinks"][j])
                kb, vb = k[:, -WINDOW:], v[:, -WINDOW:]
            else:
                o_self, kb, vb = _swa_sample(q, k, v, swa_k_in[j], swa_v_in[j], p["sinks"][j])
            new_k.append(kb)
            new_v.append(vb)
            o_self = o_self.reshape(n, t, N_Q_HEADS * HEAD_DIM)
        else:
            z = h @ p["w_in_conv"][j]
            gb = z[..., :CONV_CH]
            gc = z[..., CONV_CH:2 * CONV_CH]
            u = z[..., 2 * CONV_CH:3 * CONV_CH]
            qx = z[..., 3 * CONV_CH:]
            if is_prompt:
                prefix = jnp.zeros((n, CONV_W - 1, CONV_CH), u.dtype)
            else:
                prefix = conv_in[j]
            y, st = _causal_conv(gc * u, prefix, p["conv_w"][j])
            new_conv.append(st)
            o_self = gb * y
        qx = _rms_norm(qx.reshape(n, t, N_X_HEADS, HEAD_DIM), p["q_norm_x"][i])
        o_x = _cross_attend(qx, mem_k[i], mem_v[i]).reshape(n, t, X_DIM)
        o = jnp.concatenate([o_self, o_x.astype(o_self.dtype)], axis=-1)
        x = x + o @ p["w_out"][i]
        hm = _rms_norm(x, p["norm_mlp"][i])
        x = x + jnp.square(jax.nn.relu(hm @ p["w_up"][i])) @ p["w_down"][i]
    return x, jnp.stack(new_k), jnp.stack(new_v), jnp.stack(new_conv)

def setup_inputs(seed: int = 0) -> dict:
    key = jax.random.key(seed)
    ks = jax.random.split(key, 24)
    f32 = jnp.float32

    def nrm(k, shape, scale=1.0):
        return jax.random.normal(k, shape, f32) * scale

    def gain(k, shape):
        return 1.0 + 0.05 * jax.random.normal(k, shape, f32)

    return {
        "x_prompt": nrm(ks[0], (BATCH, SEQ, D_MODEL)),
        "x_sample": nrm(ks[1], (DEC_BATCH, DEC_SEQ, D_MODEL)),
        "mem_prompt": nrm(ks[2], (BATCH, N_MEM, D_MODEL)),
        "cache_swa_k": nrm(ks[3], (N_ATT_LAYERS, DEC_BATCH, WINDOW, N_KV_HEADS, HEAD_DIM)),
        "cache_swa_v": nrm(ks[4], (N_ATT_LAYERS, DEC_BATCH, WINDOW, N_KV_HEADS, HEAD_DIM)),
        "state_conv": nrm(ks[5], (N_CONV_LAYERS, DEC_BATCH, CONV_W - 1, CONV_CH)),
        "cache_mem_k": nrm(ks[6], (DEPTH, DEC_BATCH, N_MEM, N_X_HEADS, HEAD_DIM)),
        "cache_mem_v": nrm(ks[7], (DEPTH, DEC_BATCH, N_MEM, N_X_HEADS, HEAD_DIM)),
        "norm_mix": gain(ks[8], (DEPTH, D_MODEL)),
        "w_in_att": nrm(ks[9], (N_ATT_LAYERS, D_MODEL, ATT_IN), D_MODEL ** -0.5),
        "q_norm_att": gain(ks[10], (N_ATT_LAYERS, HEAD_DIM)),
        "k_norm_att": gain(ks[11], (N_ATT_LAYERS, HEAD_DIM)),
        "sinks": nrm(ks[12], (N_ATT_LAYERS, N_Q_HEADS), 0.5),
        "w_in_conv": nrm(ks[13], (N_CONV_LAYERS, D_MODEL, CONV_IN), D_MODEL ** -0.5),
        "conv_w": nrm(ks[14], (N_CONV_LAYERS, CONV_W, CONV_CH), CONV_W ** -0.5),
        "norm_mem": gain(ks[15], (DEPTH, D_MODEL)),
        "w_mem_kv": nrm(ks[16], (DEPTH, D_MODEL, 2 * X_DIM), D_MODEL ** -0.5),
        "q_norm_x": gain(ks[17], (DEPTH, HEAD_DIM)),
        "k_norm_x": gain(ks[18], (DEPTH, HEAD_DIM)),
        "w_out": nrm(ks[19], (DEPTH, MIX_OUT, D_MODEL), MIX_OUT ** -0.5),
        "norm_mlp": gain(ks[20], (DEPTH, D_MODEL)),
        "w_up": nrm(ks[21], (DEPTH, D_MODEL, D_FF), D_MODEL ** -0.5),
        "w_down": nrm(ks[22], (DEPTH, D_FF, D_MODEL), D_FF ** -0.5),
    }

def reference(x_prompt, x_sample, mem_prompt, cache_swa_k, cache_swa_v, state_conv, cache_mem_k, cache_mem_v,
              norm_mix, w_in_att, q_norm_att, k_norm_att, sinks, w_in_conv, conv_w, norm_mem, w_mem_kv,
              q_norm_x, k_norm_x, w_out, norm_mlp, w_up, w_down):
    p = {
        "norm_mix": norm_mix, "w_in_att": w_in_att, "q_norm_att": q_norm_att, "k_norm_att": k_norm_att,
        "sinks": sinks, "w_in_conv": w_in_conv, "conv_w": conv_w, "q_norm_x": q_norm_x,
        "w_out": w_out, "norm_mlp": norm_mlp, "w_up": w_up, "w_down": w_down,
    }
    mks, mvs = [], []
    for i in range(DEPTH):
        mk, mv = _mem_kv(mem_prompt, norm_mem[i], w_mem_kv[i], k_norm_x[i])
        mks.append(mk)
        mvs.append(mv)
    new_mem_k_prompt = jnp.stack(mks)
    new_mem_v_prompt = jnp.stack(mvs)
    y_prompt, new_swa_k_prompt, new_swa_v_prompt, new_conv_prompt = _trunk(
        x_prompt, 0.0, new_mem_k_prompt, new_mem_v_prompt, None, None, None, True, p)
    y_sample, new_swa_k_sample, new_swa_v_sample, new_conv_sample = _trunk(
        x_sample, float(PAST_LEN), cache_mem_k, cache_mem_v, cache_swa_k, cache_swa_v, state_conv, False, p)
    return (y_prompt, y_sample, new_swa_k_prompt, new_swa_v_prompt, new_conv_prompt,
            new_mem_k_prompt, new_mem_v_prompt, new_swa_k_sample, new_swa_v_sample, new_conv_sample)


_drawn_inputs = setup_inputs


def setup_inputs(seed=0):
    import zlib

    import numpy as np

    out = dict(_drawn_inputs(seed))
    spreads = {}
    factors = {'q_norm_att': 5.609, 'sinks': 8.0, 'q_norm_x': 8.0}
    for name, (base, spread) in spreads.items():
        noise = np.random.default_rng([zlib.crc32(name.encode()), seed]).standard_normal(out[name].shape)
        drawn = base * np.exp(spread * noise) if base else spread * noise
        out[name] = __import__('jax').numpy.asarray(drawn.astype(out[name].dtype))
    for name, factor in factors.items():
        out[name] = (out[name] * factor).astype(out[name].dtype)
    return out
```

```python
from contextlib import ExitStack

import numpy as np

import concourse.bass as bass
from concourse import mybir

D = 1024
SEQ = 512
SB, ST = 8, 4
NS = SB * ST
NT = SEQ + NS
HALF = NT // 2
KC = D // 128
NMEM = 256
HD = 64
NQH, NKV, NXH = 12, 4, 4
GRP = NQH // NKV
CONVC = NQH * HD // 128
FF = 4 * D
GROUPS = FF // D
PAST = 2048
EPS = 1e-6
NEG = -1e30
SCALE = HD ** -0.5
DUO = 256
Q_MEM, Q_ATT, Q_OUT0 = 0, 2, 5
Q_MLP0 = 7
Q_CONV = Q_MLP0 + 4 * GROUPS
Q_OUT1 = Q_CONV + 5
Q_MLP1 = Q_OUT1 + 2
QUADS = Q_MLP1 + 4 * GROUPS
C_G = 0
C_HG = C_G + 48
C_CW = C_HG + 6
C_SINK = C_CW + 18
C_SROW = C_SINK + 12
C_IDENT = C_SROW + 3
C_ONES = C_IDENT + 128
C_HEAD = C_ONES + 128
C_SWAP = C_HEAD + 128
C_MASKP = C_SWAP + 128
C_MASKS = C_MASKP + 256
C_BLK = C_MASKS + 132
C_ST = C_BLK + 8
C_EPS = C_ST + 96
C_ZERO = C_EPS + 1
C_N = C_ZERO + 1


def build_kernel(nc, xT, memT, wst, cst, rope, swakT, swav, xkT, xv, yT, o_kp, o_vp, o_cp, o_mk, o_mv,
                 o_ks, o_vs, o_vn, o_cs):
    f32, f32r = mybir.dt.float32, mybir.dt.float32r
    ALU, ACT = mybir.AluOpType, mybir.ActivationFunctionType
    base = [(nc.sbuf_base + 63) // 64 * 64]

    def place(name, shape, dt=f32, at=None):
        size = int(np.prod(shape[1:])) * 4
        where = base[0] if at is None else at
        if at is None:
            base[0] += (size + 31) // 32 * 32
            assert base[0] <= nc.sbuf_usable_end, (name, base[0], nc.sbuf_usable_end)
        return nc.alloc_sbuf_tensor_at(name, shape, dt, offset=where), where

    X, _ = place("x_res", [128, KC, NT])
    act_hl, at_act = [], []
    for i in range(2):
        hi, where = place(f"act{i}_hi", [128, KC, NT], f32r)
        lo, _ = place(f"act{i}_lo", [128, KC, NT], f32r)
        act_hl.append((hi, lo))
        at_act.append(where)
    z0, _ = place("z0", [128, 12, NT], at=at_act[1])
    kz, _ = place("kz", [128, NKV, SEQ], at=at_act[1] + 12 * NT * 4)
    z1, _ = place("z1", [128, 2, NT], at=at_act[0])
    vconv, _ = place("vconv", [128, CONVC, SEQ + 2], at=at_act[0] + 2 * NT * 4)
    at_s = (at_act[0] + (2 * NT + CONVC * (SEQ + 2)) * 4 + 31) // 32 * 32
    sconv, _ = place("sconv", [128, CONVC, SB, ST + 2], at=at_s)
    oconv, _ = place("oconv", [128, CONVC, NT], at=at_s + CONVC * SB * (ST + 2) * 4)
    Zs = [z0, z1]
    NORM_TO = [0, 1, 1, 0]
    stage, _ = place("w_stage", [128, 2, KC, DUO])
    w_hi, _ = place("w_hi", [128, 2, KC, DUO], f32r)
    w_lo, _ = place("w_lo", [128, 2, KC, DUO], f32r)
    rstd, _ = place("rstd", [128, NT])
    psq, _ = place("psq", [128, NT])
    pacc, _ = place("pacc", [128, NT])
    tmp, at_tmp = place("tmp", [128, 6, NT])
    qpad, _ = place("qpad", [128, 2, 144 * SB], at=at_tmp)
    con, _ = place("con", [128, C_N])
    nsink, _ = place("nsink", [128, 15])
    memkz, _ = place("memkz", [128, 2, NXH, NMEM])
    memv, _ = place("memv", [128, 2, 2, NXH * HD])
    vp, _ = place("vp", [128, 4, NKV * HD])
    vn, _ = place("vn", [128, NKV * HD])
    kt, at_kt = place("kt", [128, 2, SB, 132])
    kx, _ = place("kx", [128, 2, 4, NMEM], at=at_kt)
    memx, _ = place("memx", [128, KC, NMEM], at=at_kt)
    vb, at_vb = place("vb", [128, SB, NKV * HD])
    vx, _ = place("vx", [128, 2, 4, NXH * HD], at=at_vb)
    sm, _ = place("sm", [128, 2, 4, 256])
    pt, at_pt = place("pt", [128, 2, 2, 512])
    cs, _ = place("cs", [128, 2, NT], at=at_pt)
    st, _ = place("st", [128, 2, 5, 4])

    with ExitStack() as ctx:
        def sem(name):
            return ctx.enter_context(nc.semaphore(name))

        zps = [ctx.enter_context(nc.psum_tensor(f"zps{i}", [128, 2, 512], f32)) for i in range(2)]
        tps = ctx.enter_context(nc.psum_tensor("tps", [128, 2, 512], f32))
        ops = ctx.enter_context(nc.psum_tensor("ops", [128, 2, 512], f32))

        w_in = [sem(f"w_in{d}") for d in range(2)]
        w_his = [sem(f"w_his{d}") for d in range(2)]
        w_los = [sem(f"w_los{d}") for d in range(2)]
        z_full = [sem(f"z_full{s}") for s in range(2)]
        z_free = [sem(f"z_free{s}") for s in range(2)]
        ld = {n: sem("ld_" + n) for n in ("con", "mem", "x", "rope", "kt", "vb", "kx", "vx")}
        m_hi, m_lo = sem("m_hi"), sem("m_lo")
        a_his, a_los = sem("a_his"), sem("a_los")
        sq_acc, pool_ch = sem("sq_acc"), sem("pool_chain")
        s_full, s_sd, s_rstd = sem("s_full"), sem("s_sd"), sem("s_rstd")
        n_sq, n_ms, n_sd, n_out = (sem("n_" + s) for s in ("sq", "ms", "sd", "out"))
        r_cos, r_sw, r_out = sem("r_cos"), sem("r_sw"), sem("r_out")
        v_t, v_out = sem("v_t"), sem("v_out")
        ch = sem("dve_chain")
        u_sq, u_hi, u_lo = sem("u_sq"), sem("u_hi"), sem("u_lo")
        g_s, g_max, g_sink, g_exp, g_p, g_t, g_pt, g_o, g_ohi, g_olo = (
            sem("g_" + s) for s in ("s", "max", "sink", "exp", "p", "t", "pt", "o", "ohi", "olo"))
        qp_rdy, qp_used, kt_new, pz = sem("qp_rdy"), sem("qp_used"), sem("kt_new"), sem("pool_zero")
        kx_used, vx_used = sem("kx_used"), sem("vx_used")
        c_hi, c_lo = sem("c_hi"), sem("c_lo")
        b_out, ks_out, vs_out, stored = sem("b_out"), sem("ks_out"), sem("vs_out"), sem("stored")
        y_out, conv_done = sem("y_out"), sem("conv_done")

        ident = con[:, C_IDENT:C_IDENT + 128]
        ones = con[:, C_ONES:C_ONES + 128]
        headones = con[:, C_HEAD:C_HEAD + 128]
        swap = con[:, C_SWAP:C_SWAP + 128]
        eps = con[:, C_EPS:C_EPS + 1]

        def gain(norm, k):
            return con[:, C_G + 8 * norm + k:C_G + 8 * norm + k + 1]

        def hgain(i, a=0, b=128):
            return con[a:b, C_HG + i:C_HG + i + 1]

        def tap(j, c):
            return con[:, C_CW + 6 * j + c:C_CW + 6 * j + c + 1]

        def halves(ap2d):
            return ap2d.rearrange("p (h t) -> p h t", h=2)

        def zp(slot, n=HALF):
            return zps[slot][:, :, 0:n]

        def full(eng, q, p):
            eng.wait_ge(z_full[p % 2], q * 2 + (p // 2 + 1))

        def taken(eng, q, p):
            eng.wait_ge(z_free[p % 2], q * 2 + (p // 2 + 1))

        def next_duo(q, p):
            nq, nd = (q, 1) if p == 0 else (q + 1, 0)
            return None if isinstance(nq, int) and nq >= QUADS else (nq, nd)

        NORMS = [("mem", l, c) for l in range(2) for c in range(2)]
        N_ATT = len(NORMS)
        NORMS += [("att", 0, i) for i in range(8)]
        N_QX = [len(NORMS), len(NORMS) + 2]
        NORMS += [("qx", 0, 10), ("qx", 0, 11), ("qx", 1, 0), ("qx", 1, 1)]

        def norm_cols(n):
            return NMEM if NORMS[n][0] == "mem" else NT

        def norm_src(n):
            kind, l, i = NORMS[n]
            return tmp[:, 4, i * 256:(i + 1) * 256] if kind == "mem" else Zs[l][:, i, :]

        def norm_gain(n):
            kind, l, i = NORMS[n]
            return 4 + l if kind == "mem" else (2 + l if kind == "qx" else (1 if i < 2 else 0))

        def norm_panel(n):
            kind, l, i = NORMS[n]
            q0 = {"mem": l, "att": Q_ATT, "qx": Q_ATT if l == 0 else Q_CONV}[kind]
            return q0 + i // 4, i % 4

        GR = [("swa", blk, kv) for blk in range(SEQ // 128) for kv in range(NKV)]
        GR += [("xp", 0, h) for h in range(NXH)] + [("ss", 0, 0), ("sx", 0, 0)]
        G_L1 = len(GR)
        GR += [("xp", 1, h) for h in range(NXH)] + [("sx", 1, 0)]

        def units(j):
            return {"swa": GRP, "xp": 4, "ss": GRP, "sx": 1}[GR[j][0]]

        def width(j):
            kind, a, b = GR[j]
            return (128 if a == 0 else 256) if kind == "swa" else (132 if kind == "ss" else 256)

        def score_signal(j):
            kind, a, b = GR[j]
            if kind == "ss":
                return qp_used, 3
            if kind == "sx":
                return kx_used, 2 * (a + 1)
            return g_s, sum(k in ("swa", "xp") for k, _, _ in GR[:j + 1])

        PRODUCT, last_use, prod_need = [], [None, None], {}
        for j, (kind, a, b) in enumerate(GR):
            pair = kind in ("swa", "xp")
            banks = [(b // 2) % 2] if pair else [0, 1]
            if not pair or b % 2 == 0:
                prod_need[j] = max([last_use[k] for k in banks if last_use[k] is not None], default=None)
            if not pair or b % 2 == 1:
                for k in banks:
                    last_use[k] = len(PRODUCT)
                PRODUCT.append(j)
        P_L0 = sum(j < G_L1 for j in PRODUCT)

        def product_parts(n):
            kind, a, b = GR[PRODUCT[n]]
            hp = b // 2
            if kind == "swa":
                return [(lambda A: A[:, hp * 3:hp * 3 + 3, a * 128:(a + 1) * 128],
                         ops[:, hp % 2, 0:384].rearrange("p (g t) -> p g t", g=3))]
            if kind == "xp":
                return [(lambda A: A[:, 6 + hp, 0:SEQ], ops[:, hp % 2, 0:SEQ])]
            parts = []
            for h in range(4):
                c, r = h // 2, 64 * (h % 2)
                for g in range(GRP if kind == "ss" else 1):
                    src = ops[r:r + 64, c, g * 128:(g + 1) * 128].rearrange("p (b k t) -> p b k t", b=SB, k=4)[:, :, h, :]
                    to = c * 3 + g if kind == "ss" else 6 + c
                    parts.append((lambda A, r=r, to=to: A[r:r + 64, to, SEQ:NT].rearrange("p (b t) -> p b t", b=SB), src))
            return parts

        block = ctx.enter_context(nc.Block())

        @block.sync
        def _(sp):
            for d in range(2):
                sp.dma_start(stage[:, d], wst[d]).then_inc(w_in[d], 16)
            with sp.Fori(1, QUADS) as q:
                for d in range(2):
                    sp.wait_ge(w_los[d], q)
                    sp.dma_start(stage[:, d].rearrange("p k n -> p (k n)"),
                                 wst.rearrange("a p k n -> (a p) (k n)")[bass.ds(q * 256 + d * 128, 128), :]
                                 ).then_inc(w_in[d], 16)

        @block.tensor
        def _(pe):
            tfree, ofree = [None], [None]

            def take(cell):
                if cell[0] is not None:
                    pe.wait_ge(*cell[0])

            def panel(q, p, hi, lo, c0=0, c1=NT, ready=None, guard=True):
                d, slot, w = p // 2, p % 2, (p % 2) * 128
                if p % 2 == 0:
                    pe.wait_ge(w_los[d], q + 1)
                if guard:
                    pe.wait_ge(z_free[slot], q * 2 + p // 2)
                parts = 2 if c1 - c0 > 512 else 1
                n = (c1 - c0) // parts
                for k in range(KC):
                    if ready is not None:
                        pe.wait_ge(ready[0], ready[1] + k)
                    for i, (w_, r_) in enumerate(((w_hi, hi), (w_hi, lo), (w_lo, hi))):
                        for h in range(parts):
                            mm = pe.matmul(zps[slot][:, h, 0:n], w_[:, d, k, w:w + 128],
                                           r_[:, k, c0 + h * n:c0 + (h + 1) * n],
                                           start=(k == 0 and i == 0), stop=(k == KC - 1 and i == 2))
                mm.then_inc(z_full[slot], 1)

            def colsum(n, cols):
                pe.wait_ge(sq_acc, n)
                take(tfree)
                parts = 2 if cols > 512 else 1
                w = cols // parts
                for h in range(parts):
                    mm = pe.matmul(tps[:, h, 0:w], ones, pacc[:, h * w:(h + 1) * w], start=True, stop=True)
                mm.then_inc(s_full, 1)
                tfree[0] = (s_sd, n)

            def headsum(n):
                pe.wait_ge(n_sq, n + 1)
                take(tfree)
                parts = 2 if norm_cols(n) > 512 else 1
                w = norm_cols(n) // parts
                for h in range(parts):
                    mm = pe.matmul(tps[:, h, 0:w], headones, tmp[:, n % 2, h * w:(h + 1) * w], start=True, stop=True)
                mm.then_inc(n_ms, 1)
                tfree[0] = (n_sd, n + 1)

            def swapped(r):
                pe.wait_ge(n_out, N_ATT + r + 1)
                take(ofree)
                for h in range(2):
                    mm = pe.matmul(ops[:, h, 0:HALF], swap, z0[:, r, h * HALF:(h + 1) * HALF], start=True, stop=True)
                mm.then_inc(r_sw, 1)
                ofree[0] = (r_out, r + 1)

            def turn_memv(n):
                l, c = n // 2, n % 2
                taken(pe, Q_MEM + l, 2 + c)
                take(ofree)
                for t in range(2):
                    mm = pe.transpose(ops[:, t, 0:128], tmp[:, 5, c * 256 + t * 128:c * 256 + (t + 1) * 128], ident)
                mm.then_inc(v_t, 1)
                ofree[0] = (v_out, n + 1)

            def turn_v(c):
                taken(pe, Q_ATT + 2, c)
                take(ofree)
                for t in range(4):
                    pe.transpose(ops[:, 0, t * 128:(t + 1) * 128], z0[:, 8 + c, t * 128:(t + 1) * 128], ident)
                pe.transpose(ops[0:NS, 1, 0:128], z0[:, 8 + c, SEQ:NT], ident).then_inc(v_t, 1)
                ofree[0] = (v_out, 5 + c)

            def scores(j):
                kind, a, b = GR[j]
                s = zps[j % 2]
                if j in (0, 1, G_L1, G_L1 + 1):
                    for p in (2, 3):
                        taken(pe, (Q_OUT0 if j < G_L1 else Q_OUT1) - 1, p)
                if j >= 2:
                    pe.wait_ge(g_max, j - 1)
                if j == 0:
                    pe.wait_ge(r_out, 8)
                for u in range(units(j)):
                    out = s[:, u // 2, (u % 2) * 256:(u % 2) * 256 + width(j)]
                    if kind == "swa":
                        mm = pe.matmul(out, z0[:, 2 + (b // 2) * 3 + u, a * 128:(a + 1) * 128],
                                       kz[:, b, max(a - 1, 0) * 128:(a + 1) * 128], start=True, stop=True)
                    elif kind == "xp":
                        pe.wait_ge(n_out, N_QX[a] + 2)
                        mm = pe.matmul(out, Zs[a][:, (10 if a == 0 else 0) + b // 2, u * 128:(u + 1) * 128],
                                       memkz[:, a, b, :], start=True, stop=True)
                    elif kind == "ss":
                        pe.wait_ge(kt_new, 2)
                        pe.wait_ge(qp_rdy, u + 1)
                        for hp in range(2):
                            for bb in range(SB):
                                mm = pe.matmul(out, qpad[:, hp, bb * 128:(bb + 1) * 128], kt[:, hp, bb, :],
                                               start=(hp == 0 and bb == 0), stop=(hp == 1 and bb == SB - 1))
                        mm.then_inc(qp_used, 1)
                    else:
                        pe.wait_ge(qp_rdy, 4 + a)
                        for hb in range(2):
                            pe.wait_ge(ld["kx"], 16 * (2 * a + hb + 1))
                            for hp in range(2):
                                for bb in range(4):
                                    c = (hb * 4 + bb) * 128
                                    mm = pe.matmul(out, qpad[:, hp, c:c + 128], kx[:, hp, bb, :],
                                                   start=(hb == 0 and hp == 0 and bb == 0),
                                                   stop=(hb == 1 and hp == 1 and bb == 3))
                            mm.then_inc(kx_used, 1)
                if kind in ("swa", "xp"):
                    mm.then_inc(g_s, 1)

            def turn_p(j):
                pe.wait_ge(g_p, j + 1)
                take(tfree)
                for u in range(units(j)):
                    for t in range(width(j) // 128):
                        mm = pe.transpose(tps[:, t, u * 128:(u + 1) * 128], sm[:, j % 2, u, t * 128:(t + 1) * 128], ident)
                    if GR[j][0] == "ss":
                        mm = pe.transpose(tps[0:NS, 1, u * 128:(u + 1) * 128], sm[:, j % 2, u, 160:192], ident)
                mm.then_inc(g_t, 1)
                tfree[0] = (g_pt, j + 1)

            def values(j):
                kind, a, b = GR[j]
                pe.wait_ge(g_pt, j + 1)
                if j in (0, 1, G_L1, G_L1 + 1):
                    take(ofree)
                if prod_need.get(j) is not None:
                    pe.wait_ge(g_olo, prod_need[j] + 1)
                probs = pt[:, j % 2]
                r = 64 * (b % 2)
                if kind == "swa":
                    tiles = [0] if a == 0 else [a - 1, a]
                    for i, t in enumerate(tiles):
                        mm = pe.matmul(ops[r:r + 64, (b // 2) % 2, 0:384], vp[:, t, b * 64:(b + 1) * 64],
                                       probs[:, i, 0:384], start=(i == 0), stop=(i == len(tiles) - 1))
                elif kind == "xp":
                    for i in range(2):
                        mm = pe.matmul(ops[r:r + 64, (b // 2) % 2, 0:SEQ], memv[:, a, i, b * 64:(b + 1) * 64],
                                       probs[:, i, :], start=(i == 0), stop=(i == 1))
                elif kind == "ss":
                    pe.wait_ge(ld["vb"], 16)
                    for hp in range(2):
                        pe.matmul(ops[:, hp, 0:384], vn[0:NS, hp * 128:(hp + 1) * 128], probs[0:NS, 1, 0:384],
                                  start=True, stop=False, skip_group_check=True)
                        for bb in range(SB):
                            o = ops[:, hp, 0:384].rearrange("p (g r) -> p g r", g=3)[:, :, bb * 16:(bb + 1) * 16]
                            m = probs[:, 0, 0:384].rearrange("p (g r) -> p g r", g=3)[:, :, bb * 16:(bb + 1) * 16]
                            mm = pe.matmul(o, vb[:, bb, hp * 128:(hp + 1) * 128], m,
                                           start=False, stop=(bb == SB - 1), skip_group_check=True)
                else:
                    for hb in range(2):
                        pe.wait_ge(ld["vx"], 16 * (2 * a + hb + 1))
                        for bb in range(4):
                            c = (hb * 4 + bb) * 16
                            for hp in range(2):
                                for t in range(2):
                                    mm = pe.matmul(ops[:, hp, c:c + 16], vx[:, t, bb, hp * 128:(hp + 1) * 128],
                                                   probs[:, t, c:c + 16], start=(t == 0), stop=(t == 1))
                        if hb == 0:
                            mm.then_inc(vx_used, 1)
                if j in PRODUCT:
                    mm.then_inc(g_o, 1)

            def attention(j0, j1):
                for j in range(j0, j1 + 2):
                    if j < j1:
                        scores(j)
                    if j0 <= j - 1 < j1:
                        turn_p(j - 1)
                    if j0 <= j - 2 < j1:
                        values(j - 2)

            def out_proj(q0, l, need):
                for sem_, value in need:
                    pe.wait_ge(sem_, value)
                for m in range(8):
                    panel(q0 + m // 4, m % 4, *act_hl[l])

            def mlp_group(q, l, u0, first=None, stat=None):
                for m in range(8):
                    panel(q + m // 4, m % 4, *act_hl[1 - l], ready=first if m == 0 else None)
                    if m == 0 and stat:
                        colsum(stat, NT)
                for m in range(8):
                    panel(q + (2 + m // 4), m % 4, *act_hl[l], ready=(u_lo, u0 + 1) if m == 0 else None)

            def mlp(q0, l, first, stat):
                mlp_group(q0, l, 32 * l, first, stat)
                with pe.Fori(1, GROUPS) as g:
                    mlp_group(g * 4 + q0, l, g * 8 + 32 * l)

            pe.wait_ge(ld["con"], 16)
            for l in range(2):
                for p in range(4):
                    panel(Q_MEM + l, p, *act_hl[1], l * NMEM, (l + 1) * NMEM,
                          ready=(m_lo, 8 * l + 1) if p == 0 else None, guard=l > 0 or p >= 2)
                    if (l, p) == (0, 0):
                        colsum(1, NMEM)
                    if p in (1, 2):
                        headsum(2 * l + p - 1)
                    if p == 3:
                        turn_memv(2 * l)
                    if (l, p) == (1, 0):
                        turn_memv(1)
            for i in range(12):
                panel(Q_ATT + i // 4, i % 4, *act_hl[0], ready=(a_los, 1) if i == 0 else None)
                if i == 0:
                    turn_memv(3)
                    colsum(2, NT)
                if 1 <= i <= 8:
                    headsum(N_ATT + i - 1)
                if 2 <= i <= 9:
                    swapped(i - 2)
                if i >= 10:
                    turn_v(i - 10)
                if i == 11:
                    headsum(N_QX[0])
            headsum(N_QX[0] + 1)
            attention(0, G_L1)
            out_proj(Q_OUT0, 0, [(g_olo, P_L0)])
            mlp(Q_MLP0, 0, (a_los, 9), 3)
            for i in range(20):
                panel(Q_CONV + i // 4, i % 4, *act_hl[1], ready=(a_los, 17) if i == 0 else None)
                if i == 0:
                    colsum(4, NT)
                if i in (1, 2):
                    headsum(N_QX[1] + i - 1)
            attention(G_L1, len(GR))
            out_proj(Q_OUT1, 1, [(g_olo, len(PRODUCT)), (c_lo, CONVC)])
            mlp(Q_MLP1, 1, (a_los, 25), 5)

        @block.vector
        def _(dve):
            chained = [0]

            def link(ins):
                chained[0] += 1
                ins.then_inc(ch, 1)
                dve.wait_ge(ch, chained[0])

            def split_lo(q, d):
                dve.wait_ge(w_his[d], q + 1)
                dve.tensor_tensor(w_lo[:, d], stage[:, d], w_hi[:, d].bitcast(f32), ALU.subtract).then_inc(w_los[d], 1)

            def split_next(q, p):
                if p % 2 == 0 and next_duo(q, p):
                    split_lo(*next_duo(q, p))

            def take_scaled(q, p, out, cols=NT):
                full(dve, q, p)
                if cols > 512:
                    ins = dve.tensor_tensor(halves(out), zp(p % 2), halves(rstd[:, :]), ALU.mult)
                else:
                    ins = dve.tensor_tensor(out, zps[p % 2][:, 0, 0:cols], rstd[:, 0:cols], ALU.mult)
                ins.then_inc(z_free[p % 2], 1)

            def inv_rms(n, cols):
                dve.wait_ge(s_sd, n)
                dve.reciprocal(rstd[:, 0:cols], tmp[:, 2, 0:cols]).then_inc(s_rstd, 1)
                dve.wait_ge(s_rstd, n)

            def head_norm(n):
                kind, l, i = NORMS[n]
                cols = norm_cols(n)
                dve.wait_ge(n_sd, n + 1)
                taken(dve, *norm_panel(n))
                link(dve.reciprocal(tmp[:, 3, 0:cols], tmp[:, 2, 0:cols]))
                src = norm_src(n)
                if kind == "mem":
                    for hf in range(2):
                        r = slice(64 * hf, 64 * hf + 64)
                        ins = dve.scalar_tensor_tensor(out=memkz[r, l, 2 * i + hf, :], in0=src[r],
                                                       scalar=hgain(norm_gain(n), r.start, r.stop),
                                                       in1=tmp[r, 3, 0:cols], op0=ALU.mult, op1=ALU.mult)
                else:
                    ins = dve.scalar_tensor_tensor(out=src, in0=src, scalar=hgain(norm_gain(n)), in1=tmp[:, 3, :],
                                                   op0=ALU.mult, op1=ALU.mult)
                ins.then_inc(n_out, 1)

            def rotate(r):
                dve.wait_ge(r_sw, r + 1)
                link(dve.tensor_tensor(halves(tmp[:, 5, :]), ops[:, :, 0:HALF], halves(cs[:, 1, :]), ALU.mult))
                dve.wait_ge(r_cos, r + 1)
                ins = dve.tensor_tensor(z0[:, r, :], tmp[:, 4, :], tmp[:, 5, :], ALU.add)
                if r < 2:
                    link(ins)
                    for hf in range(2):
                        s = slice(64 * hf, 64 * hf + 64)
                        ins = dve.tensor_copy(kz[s, 2 * r + hf, :], z0[s, r, 0:SEQ])
                ins.then_inc(r_out, 1)

            def turned_v(n):
                dve.wait_ge(v_t, n + 1)
                if n < 4:
                    l, c = n // 2, n % 2
                    dve.tensor_copy(memv[:, l, :, c * 128:(c + 1) * 128], ops[:, :, 0:128]).then_inc(v_out, 1)
                else:
                    c = n - 4
                    link(dve.tensor_copy(vp[:, :, c * 128:(c + 1) * 128], ops[:, 0, :].rearrange("p (t d) -> p t d", t=4)))
                    dve.tensor_copy(vn[0:NS, c * 128:(c + 1) * 128], ops[0:NS, 1, 0:128]).then_inc(v_out, 1)

            def norm_lo(n, k, norm):
                dve.wait_ge(a_his, 8 * n + k + 1)
                hi, lo = act_hl[NORM_TO[n]]
                dve.scalar_tensor_tensor(out=lo[:, k, :], in0=X[:, k, :], scalar=gain(norm, k),
                                         in1=hi[:, k, :].bitcast(f32), op0=ALU.mult, op1=ALU.subtract).then_inc(a_los, 1)

            def residual(q, m):
                p = m % 4
                full(dve, q + m // 4, p)
                dve.wait_ge(z_free[p % 2], (q + m // 4) * 2 + p // 2)
                dve.tensor_tensor(halves(X[:, m, :]), zp(p % 2), halves(X[:, m, :]), ALU.add).then_inc(z_free[p % 2], 1)

            def maxes(j):
                kind, a, b = GR[j]
                w = width(j)
                dve.wait_ge(*score_signal(j))
                if j >= 2:
                    dve.wait_ge(g_t, j - 1)
                for u in range(units(j)):
                    s = zps[j % 2][:, u // 2, (u % 2) * 256:(u % 2) * 256 + w]
                    if kind == "swa":
                        mask, first = con[:, C_MASKP + 256 - w:C_MASKP + 256], nsink[:, b * 3 + u:b * 3 + u + 1]
                    elif kind == "ss":
                        mask, first = con[:, C_MASKS:C_MASKS + 132], nsink[:, 12 + u:13 + u]
                    else:
                        mask, first = con[:, C_ZERO:C_ZERO + 1].broadcast_to([128, w]), 3.0e38
                    ins = dve.tensor_tensor_reduce(out=sm[:, j % 2, u, 0:w], in0=s, in1=mask, scale=-SCALE, scalar=first,
                                                   op0=ALU.add, op1=ALU.min, accum_out=st[:, j % 2, 0, u:u + 1])
                ins.then_inc(g_max, 1)
                if kind in ("swa", "ss"):
                    n0 = b * 3 if kind == "swa" else 12
                    dve.wait_ge(g_max, j + 1)
                    dve.tensor_tensor(st[:, j % 2, 2, 0:3], st[:, j % 2, 0, 0:3], nsink[:, n0:n0 + 3],
                                      ALU.subtract).then_inc(g_sink, 1)

            def normalise(j):
                kind = GR[j][0]
                n, w, b = units(j), width(j), j % 2
                dve.wait_ge(g_exp, j + 1)
                total = st[:, b, 1, 0:n]
                if kind in ("swa", "ss"):
                    link(dve.tensor_tensor(st[:, b, 3, 0:n], total, st[:, b, 2, 0:n], ALU.add))
                    total = st[:, b, 3, 0:n]
                link(dve.reciprocal(st[:, b, 4, 0:n], total))
                for u in range(n):
                    ins = dve.tensor_scalar(sm[:, b, u, 0:w], sm[:, b, u, 0:w], st[:, b, 4, u:u + 1], None, ALU.mult)
                if kind == "ss":
                    link(ins)
                    for u in range(n):
                        own = sm[:, b, u, 128:132].unsqueeze(1).broadcast_to([128, SB, ST])
                        blk = con[:, C_BLK:C_BLK + SB].unsqueeze(2).broadcast_to([128, SB, ST])
                        ins = dve.tensor_tensor(sm[:, b, u, 160:192].rearrange("p (b t) -> p b t", b=SB), own, blk, ALU.mult)
                ins.then_inc(g_p, 1)

            def product_lo(n):
                dve.wait_ge(g_ohi, n + 1)
                hi, lo = act_hl[n >= P_L0]
                for dst, src in product_parts(n):
                    ins = dve.tensor_tensor(dst(lo), src, dst(hi).bitcast(f32), ALU.subtract)
                ins.then_inc(g_olo, 1)

            def attention(j0, j1):
                for j in range(j0, j1 + 3):
                    if j < j1:
                        maxes(j)
                    if j0 <= j - 1 < j1:
                        normalise(j - 1)
                    if j0 <= j - 3 < j1 and j - 3 in PRODUCT:
                        product_lo(PRODUCT.index(j - 3))

            def out_proj(q0, n, norm):
                for m in range(8):
                    split_next(q0 + m // 4, m % 4)
                    residual(q0, m)
                    taken(dve, q0 + m // 4, m % 4)
                    norm_lo(n, m, norm)

            def hidden_lo(l, u, m):
                dve.wait_ge(u_hi, u + 1)
                hi, lo = act_hl[l]
                dve.tensor_tensor(lo[:, m, :], tmp[:, 3 + m % 2, :], hi[:, m, :].bitcast(f32),
                                  ALU.subtract).then_inc(u_lo, 1)

            def mlp_group(q, l, u0, first=False, stat=None, then=None):
                for m in range(8):
                    split_next(q + m // 4, m % 4)
                    full(dve, q + m // 4, m % 4)
                    if m == 0 and stat:
                        inv_rms(stat, NT)
                    if m >= 2 or not first:
                        dve.wait_ge(u_sq, u0 + (m - 1))
                    dve.scalar_tensor_tensor(out=halves(tmp[:, m % 2, :]), in0=zp(m % 2), scalar=0.0,
                                             in1=halves(rstd[:, :]), op0=ALU.max, op1=ALU.mult).then_inc(z_free[m % 2], 1)
                    if m >= 1:
                        hidden_lo(l, u0 + (m - 1), m - 1)
                hidden_lo(l, u0 + 7, 7)
                for m in range(8):
                    split_next(q + (2 + m // 4), m % 4)
                    residual(q + 2, m)
                    if then:
                        taken(dve, q + 2 + m // 4, m % 4)
                        norm_lo(then[0], m, then[1])

            def mlp(q0, l, stat, then):
                mlp_group(q0, l, 32 * l, first=l == 0, stat=stat)
                with dve.Fori(1, GROUPS - 1) as g:
                    mlp_group(g * 4 + q0, l, g * 8 + 32 * l)
                mlp_group(q0 + 4 * (GROUPS - 1), l, 32 * l + 8 * (GROUPS - 1), then=then)

            dve.wait_ge(ld["con"], 16)
            link(dve.tensor_scalar(nsink[:, :], con[:, C_SINK:C_SINK + 15], -1.0, None, ALU.mult))
            link(dve.memset(memkz[:, :, :, :], 0.0))
            split_lo(0, 0)
            for l in range(2):
                for k in range(KC):
                    cols = slice(l * NMEM, (l + 1) * NMEM)
                    dve.wait_ge(m_hi, 8 * l + k + 1)
                    dve.scalar_tensor_tensor(out=act_hl[1][1][:, k, cols], in0=memx[:, k, :], scalar=gain(4 + l, k),
                                             in1=act_hl[1][0][:, k, cols].bitcast(f32), op0=ALU.mult,
                                             op1=ALU.subtract).then_inc(m_lo, 1)
                if l == 0:
                    inv_rms(1, NMEM)
            for l in range(2):
                for p in range(4):
                    q = Q_MEM + l
                    split_next(q, p)
                    take_scaled(q, p, tmp[:, 4 + p // 2, (p % 2) * 256:(p % 2) * 256 + 256], NMEM)
                    if l == 0:
                        for k in (2 * p, 2 * p + 1):
                            norm_lo(0, k, 0)
                    if p in (1, 2):
                        head_norm(2 * l + p - 1)
                    if p == 3:
                        turned_v(2 * l)
                    if (l, p) == (1, 0):
                        turned_v(1)
            for i in range(12):
                q, p = Q_ATT + i // 4, i % 4
                split_next(q, p)
                if i == 0:
                    turned_v(3)
                    inv_rms(2, NT)
                take_scaled(q, p, z0[:, i, :])
                if i == 0:
                    dve.wait_ge(ld["rope"], 16)
                    link(dve.memset(kz[:, :, :], 0.0))
                if 1 <= i <= 8:
                    head_norm(N_ATT + i - 1)
                if 2 <= i <= 9:
                    rotate(i - 2)
                if i >= 10:
                    turned_v(4 + i - 10)
                if i == 11:
                    head_norm(N_QX[0])
            head_norm(N_QX[0] + 1)
            attention(0, G_L1)
            dve.wait_ge(b_out, 16)
            out_proj(Q_OUT0, 1, 2)
            mlp(Q_MLP0, 0, 3, (2, 1))
            for i in range(20):
                q, p = Q_CONV + i // 4, i % 4
                split_next(q, p)
                if i == 0:
                    inv_rms(4, NT)
                if i < 2:
                    take_scaled(q, p, z1[:, i, :])
                else:
                    c, what = (i - 2) // 3, (i - 2) % 3
                    take_scaled(q, p, tmp[:, 4 if what != 1 else 5, :])
                    taken(dve, q, p)
                    if what == 1:
                        if c == 0:
                            link(dve.memset(vconv[:, :, 0:2], 0.0))
                            link(dve.tensor_copy(sconv[:, :, :, 0:2], con[:, C_ST:C_ST + 96].rearrange(
                                "p (c b t) -> p c b t", c=CONVC, b=SB)))
                        by_b = (lambda ap: ap.rearrange("p (b t) -> p b t", b=SB))
                        dve.tensor_tensor(vconv[:, c, 2:SEQ + 2], tmp[:, 4, 0:SEQ], tmp[:, 5, 0:SEQ], ALU.mult)
                        link(dve.tensor_tensor(sconv[:, c, :, 2:ST + 2], by_b(tmp[:, 4, SEQ:NT]), by_b(tmp[:, 5, SEQ:NT]), ALU.mult))
                        y, ys = tmp[:, 0, 0:SEQ], by_b(tmp[:, 0, SEQ:NT])
                        dve.tensor_scalar(y, vconv[:, c, 0:SEQ], tap(0, c), None, ALU.mult)
                        link(dve.tensor_scalar(ys, sconv[:, c, :, 0:ST], tap(0, c), None, ALU.mult))
                        for j in (1, 2):
                            dve.scalar_tensor_tensor(out=y, in0=vconv[:, c, j:SEQ + j], scalar=tap(j, c), in1=y,
                                                     op0=ALU.mult, op1=ALU.add)
                            link(dve.scalar_tensor_tensor(out=ys, in0=sconv[:, c, :, j:ST + j], scalar=tap(j, c), in1=ys,
                                                          op0=ALU.mult, op1=ALU.add))
                    if what == 2:
                        link(dve.tensor_tensor(oconv[:, c, :], tmp[:, 4, :], tmp[:, 0, :], ALU.mult))
                if i in (1, 2):
                    head_norm(N_QX[1] + i - 1)
            dve.memset(nsink[:, 0:1], 0.0).then_inc(conv_done, 1)
            for c in range(CONVC):
                dve.wait_ge(c_hi, c + 1)
                dve.tensor_tensor(act_hl[1][1][:, c, :], oconv[:, c, :], act_hl[1][0][:, c, :].bitcast(f32), ALU.subtract).then_inc(c_lo, 1)
            attention(G_L1, len(GR))
            dve.wait_ge(b_out, 48)
            out_proj(Q_OUT1, 3, 3)
            mlp(Q_MLP1, 1, 5, None)

        @block.scalar
        def _(act):
            sd_free = [None]

            def copy(out, in_, **kw):
                return act.activation(out, in_, ACT.Copy, **kw)

            def split_hi(q, d, first=False):
                act.wait_ge(w_in[d], q * 16 + 16)
                if not first:
                    act.wait_ge(z_full[1], q * 2 + (d - 1))
                copy(w_hi[:, d], stage[:, d]).then_inc(w_his[d], 1)

            def split_next(q, p):
                if p % 2 == 0 and next_duo(q, p):
                    split_hi(*next_duo(q, p), first=isinstance(q, int) and next_duo(q, p)[0] == 0)

            def root(src, dst, mean_of, sem_in, n, sem_out, free):
                act.wait_ge(sem_in, n)
                if sd_free[0]:
                    act.wait_ge(*sd_free[0])
                act.activation(dst, src, ACT.Sqrt, bias=eps, scale=1.0 / mean_of).then_inc(sem_out, 1)
                sd_free[0] = free

            def root_tokens(n, cols):
                src, dst = (tps[:, :, 0:HALF], halves(tmp[:, 2, :])) if cols > 512 else (tps[:, 0, 0:cols], tmp[:, 2, 0:cols])
                root(src, dst, D, s_full, n, s_sd, (s_rstd, n))

            def root_heads(n):
                cols = norm_cols(n)
                src, dst = (tps[:, :, 0:HALF], halves(tmp[:, 2, :])) if cols > 512 else (tps[:, 0, 0:cols], tmp[:, 2, 0:cols])
                root(src, dst, HD, n_ms, n + 1, n_sd, (n_out, n + 1))

            def square(n):
                taken(act, *norm_panel(n))
                if n >= 2:
                    act.wait_ge(n_ms, n - 1)
                act.activation(tmp[:, n % 2, 0:norm_cols(n)], norm_src(n), ACT.Square).then_inc(n_sq, 1)

            def norm_hi(n, k, norm):
                copy(act_hl[NORM_TO[n]][0][:, k, :], X[:, k, :], scale=gain(norm, k)).then_inc(a_his, 1)

            def exps(j):
                kind = GR[j][0]
                b, n, w = j % 2, units(j), width(j)
                act.wait_ge(g_max, j + 1)
                for u in range(n):
                    ins = act.activation(sm[:, b, u, 0:w], sm[:, b, u, 0:w], ACT.Exp, bias=st[:, b, 0, u:u + 1],
                                         scale=-1.0, accum_out=st[:, b, 1, u:u + 1])
                if kind in ("swa", "ss"):
                    act.wait_ge(g_sink, sum(k in ("swa", "ss") for k, _, _ in GR[:j + 1]))
                    ins = act.activation(st[:, b, 2, 0:3], st[:, b, 2, 0:3], ACT.Exp)
                ins.then_inc(g_exp, 1)

            def probs_out(j):
                kind, b = GR[j][0], j % 2
                act.wait_ge(g_t, j + 1)
                n = units(j) * 128
                if kind == "ss":
                    copy(pt[:, b, 0, 0:n], tps[:, 0, 0:n])
                    ins = copy(pt[0:NS, b, 1, 0:n], tps[0:NS, 1, 0:n])
                elif width(j) == 128:
                    ins = copy(pt[:, b, 0, 0:n], tps[:, 0, 0:n])
                else:
                    ins = copy(pt[:, b, :, 0:n], tps[:, :, 0:n])
                ins.then_inc(g_pt, 1)

            def product_hi(n):
                act.wait_ge(g_o, n + 1)
                for dst, src in product_parts(n):
                    ins = copy(dst(act_hl[n >= P_L0][0]), src)
                ins.then_inc(g_ohi, 1)

            def attention(j0, j1):
                for j in range(j0, j1 + 3):
                    if j < j1:
                        exps(j)
                    if j0 <= j - 1 < j1:
                        probs_out(j - 1)
                    if j0 <= j - 2 < j1 and j - 2 in PRODUCT:
                        product_hi(PRODUCT.index(j - 2))

            def out_proj(q0, n, norm):
                for m in range(8):
                    split_next(q0 + m // 4, m % 4)
                    taken(act, q0 + m // 4, m % 4)
                    norm_hi(n, m, norm)

            def mlp_group(q, l, u0, first=False, stat=None, then=None, last=False):
                for m in range(8):
                    split_next(q + m // 4, m % 4)
                    if m == 0 and stat:
                        root_tokens(stat, NT)
                    taken(act, q + m // 4, m % 4)
                    if m >= 2 or not first:
                        act.wait_ge(u_lo, u0 + (m - 1))
                    act.activation(tmp[:, 3 + m % 2, :], tmp[:, m % 2, :], ACT.Square).then_inc(u_sq, 1)
                    act.wait_ge(u_sq, u0 + (m + 1))
                    copy(act_hl[l][0][:, m, :], tmp[:, 3 + m % 2, :]).then_inc(u_hi, 1)
                for m in range(8):
                    split_next(q + (2 + m // 4), m % 4)
                    if then is not None:
                        taken(act, q + 2 + m // 4, m % 4)
                        norm_hi(then[0], m, then[1])
                    if last:
                        taken(act, q + 2 + m // 4, m % 4)
                        act.dma_start(yT[:, m, :], X[:, m, :]).then_inc(y_out, 16)

            def mlp(q0, l, stat, then, last):
                mlp_group(q0, l, 32 * l, first=l == 0, stat=stat)
                with act.Fori(1, GROUPS - 1) as g:
                    mlp_group(g * 4 + q0, l, g * 8 + 32 * l)
                mlp_group(q0 + 4 * (GROUPS - 1), l, 32 * l + 8 * (GROUPS - 1), then=then, last=last)

            act.dma_start(con[:, :], cst).then_inc(ld["con"], 16)
            act.dma_start(memx[:, :, :], memT).then_inc(ld["mem"], 16)
            act.dma_start(X[:, :, :], xT).then_inc(ld["x"], 16)
            act.dma_start(cs[:, :, :], rope).then_inc(ld["rope"], 16)
            act.wait_ge(ld["con"], 16)
            act.wait_ge(ld["mem"], 16)
            for l in range(2):
                for k in range(KC):
                    copy(act_hl[1][0][:, k, l * NMEM:(l + 1) * NMEM], memx[:, k, :], scale=gain(4 + l, k)).then_inc(m_hi, 1)
                if l == 0:
                    split_hi(0, 0, first=True)
                    root_tokens(1, NMEM)
            act.wait_ge(ld["x"], 16)
            for l in range(2):
                for p in range(4):
                    split_next(Q_MEM + l, p)
                    if l == 0:
                        for k in (2 * p, 2 * p + 1):
                            norm_hi(0, k, 0)
                    if p < 2:
                        square(2 * l + p)
                    if p in (1, 2):
                        root_heads(2 * l + p - 1)
            for i in range(12):
                split_next(Q_ATT + i // 4, i % 4)
                if i == 0:
                    root_tokens(2, NT)
                if i < 8:
                    square(N_ATT + i)
                if i >= 10:
                    square(N_QX[0] + i - 10)
                if 1 <= i <= 8:
                    root_heads(N_ATT + i - 1)
                if i == 11:
                    root_heads(N_QX[0])
            root_heads(N_QX[0] + 1)
            attention(0, G_L1)
            act.wait_ge(b_out, 16)
            out_proj(Q_OUT0, 1, 2)
            mlp(Q_MLP0, 0, 3, (2, 1), False)
            for i in range(20):
                split_next(Q_CONV + i // 4, i % 4)
                if i == 0:
                    root_tokens(4, NT)
                if i < 2:
                    square(N_QX[1] + i)
                if i in (1, 2):
                    root_heads(N_QX[1] + i - 1)
            act.wait_ge(conv_done, 1)
            for c in range(CONVC):
                copy(act_hl[1][0][:, c, :], oconv[:, c, :]).then_inc(c_hi, 1)
            attention(G_L1, len(GR))
            act.wait_ge(b_out, 48)
            out_proj(Q_OUT1, 3, 3)
            mlp(Q_MLP1, 1, 5, None, True)
            act.wait_ge(y_out, 16 * 8)

        @block.gpsimd
        def _(pool):
            n_chain = [0]

            def link(ins):
                n_chain[0] += 1
                ins.then_inc(pool_ch, 1)
                pool.wait_ge(pool_ch, n_chain[0])

            def sum_squares(n, src, cols, before):
                if n > 1:
                    pool.wait_ge(s_full, n - 1)
                for k in range(KC):
                    before(k)
                    x = src[:, k, 0:cols]
                    if k == 0:
                        link(pool.tensor_tensor(pacc[:, 0:cols], x, x, ALU.mult))
                        continue
                    link(pool.tensor_tensor(psq[:, 0:cols], x, x, ALU.mult))
                    ins = pool.tensor_tensor(pacc[:, 0:cols], pacc[:, 0:cols], psq[:, 0:cols], ALU.add)
                    if k < KC - 1:
                        link(ins)
                ins.then_inc(sq_acc, 1)
                pool.wait_ge(sq_acc, n)

            def spread_queries(src, n):
                for h in range(4):
                    r = slice(64 * (h % 2), 64 * (h % 2) + 64)
                    dst = qpad[r, h // 2, :].rearrange("p (b r) -> p b r", r=144)[:, :, h * 4:h * 4 + 4]
                    ins = pool.tensor_copy(dst, src(h // 2)[r, SEQ:NT].rearrange("p (b t) -> p b t", b=SB))
                ins.then_inc(qp_rdy, 1)

            def load_cross(l):
                for hb in range(2):
                    if hb == 0:
                        pool.wait_ge(*((qp_used, 3) if l == 0 else (kx_used, 2)))
                        if l == 0:
                            pool.wait_ge(ks_out, 16)
                    else:
                        pool.wait_ge(kx_used, 2 * l + 1)
                    pool.dma_start(kx[:, :, :, :], xkT[l, hb]).then_inc(ld["kx"], 16)
                    if l == 1 and hb == 0:
                        pool.wait_ge(g_o, P_L0)
                        pool.dma_start(vx[:, :, :, :], xv[l, 0]).then_inc(ld["vx"], 16)
                        yield
                if l == 0:
                    pool.wait_ge(g_o, P_L0 - 1)
                    pool.wait_ge(vs_out, 32)
                    pool.dma_start(vx[:, :, :, :], xv[l, 0]).then_inc(ld["vx"], 16)
                pool.wait_ge(vx_used, l + 1)
                pool.dma_start(vx[:, :, :, :], xv[l, 1]).then_inc(ld["vx"], 16)
                yield

            pool.wait_ge(ld["mem"], 16)
            sum_squares(1, memx, NMEM, lambda k: None)
            pool.wait_ge(ld["x"], 16)
            sum_squares(2, X, NT, lambda k: None)
            pool.dma_start(vb[:, :, :], swav).then_inc(ld["vb"], 16)
            pool.wait_ge(m_lo, 16)
            pool.wait_ge(m_hi, 16)
            pool.dma_start(kt[:, :, :, 0:128], swakT).then_inc(ld["kt"], 16)
            pool.wait_ge(ld["rope"], 16)
            for r in range(8):
                pool.wait_ge(n_out, N_ATT + r + 1)
                if r:
                    pool.wait_ge(r_out, r)
                pool.tensor_tensor(tmp[:, 4, :], z0[:, r, :], cs[:, 0, :], ALU.mult).then_inc(r_cos, 1)
            pool.wait_ge(ld["kt"], 16)
            for hp in range(2):
                pool.wait_ge(r_out, 8)
                pool.tensor_copy(kt[:, hp, :, 128:132], z0[:, hp, SEQ:NT].rearrange("p (b t) -> p b t", b=SB)).then_inc(kt_new, 1)
            pool.wait_ge(kt_new, 2)
            pool.wait_ge(n_out, N_QX[0] + 2)
            pool.memset(qpad[:, :, :], 0.0).then_inc(pz, 1)
            pool.wait_ge(pz, 1)
            spread_queries(lambda hp: z0[:, 2 + hp * 3, :], 0)
            pool.dma_start(o_kp, z0[:, 0:2, SEQ - 128:SEQ]).then_inc(b_out, 16)
            pool.dma_start(o_ks, kt[:, :, :, ST:132]).then_inc(ks_out, 16)
            pool.wait_ge(v_out, 6)
            pool.wait_ge(ld["vb"], 16)
            pool.dma_start(o_vp, vp[:, 3, :]).then_inc(stored, 16)
            pool.dma_start(o_vs.rearrange("b s d -> s b d"), vb[ST:128, :, :]).then_inc(vs_out, 16)
            pool.dma_start(o_vn, vn[0:NS, :]).then_inc(vs_out, 16)
            for l in range(2):
                for h in range(NXH):
                    r = slice(64 * (h % 2), 64 * (h % 2) + 64)
                    pool.dma_start(o_mk[l, h], memkz[r, l, h, :]).then_inc(stored, 16)
                pool.dma_start(o_mv[l], memv[:, l, :, :]).then_inc(stored, 16)
            for g in range(1, GRP):
                pool.wait_ge(qp_used, g)
                spread_queries(lambda hp: z0[:, 2 + hp * 3 + g, :], g)
            pool.wait_ge(qp_used, GRP)
            spread_queries(lambda hp: z0[:, 10 + hp, :], 3)
            for _ in load_cross(0):
                pass
            pool.wait_ge(g_o, P_L0)
            cross1 = load_cross(1)
            next(cross1)
            sum_squares(3, X, NT, lambda k: taken(pool, Q_OUT0 + k // 4, k % 4))
            sum_squares(4, X, NT, lambda k: taken(pool, Q_CONV - 2 + k // 4, k % 4))
            pool.wait_ge(conv_done, 1)
            pool.dma_start(o_cp, vconv[:, :, SEQ:SEQ + 2]).then_inc(b_out, 16)
            pool.dma_start(o_cs, sconv[:, :, :, ST:ST + 2]).then_inc(b_out, 16)
            pool.wait_ge(n_out, N_QX[1] + 2)
            pool.memset(qpad[:, :, :], 0.0).then_inc(pz, 1)
            pool.wait_ge(pz, 2)
            spread_queries(lambda hp: z1[:, hp, :], 4)
            for _ in cross1:
                pass
            sum_squares(5, X, NT, lambda k: taken(pool, Q_OUT1 + k // 4, k % 4))
            pool.wait_ge(stored, 16 * 11)


def kernel(**inputs):
    from concourse import bacc
    from concourse.bass_utils import run_bass_kernel_spmd

    x = {k: np.asarray(v) for k, v in inputs.items()}

    def duos(w):
        return w.reshape(KC, 128, -1, DUO).transpose(2, 1, 0, 3)

    def feat(a):
        return a.reshape(-1, KC, 128).transpose(2, 1, 0)

    order = [(2 * hp + hf) * GRP + g for hp in range(2) for g in range(GRP) for hf in range(2)]
    qcols = np.concatenate([np.arange(h * HD, (h + 1) * HD) for h in order])
    c0, c1, c2 = NQH * HD, (NQH + NKV) * HD, (NQH + 2 * NKV) * HD
    wa = x["w_in_att"][0]
    parts = [x["w_mem_kv"][0], x["w_mem_kv"][1],
             np.concatenate([wa[:, c0:c1], wa[:, qcols], wa[:, c1:]], axis=1),
             np.concatenate([x["w_out"][0][qcols], x["w_out"][0][c0:]], axis=0)]

    def mlp(l):
        for g in range(GROUPS):
            parts.append(x["w_up"][l][:, g * D:(g + 1) * D])
            parts.append(x["w_down"][l][g * D:(g + 1) * D])

    mlp(0)
    wc = x["w_in_conv"][0]
    cc = CONVC * 128
    cols = [wc[:, 3 * cc:]]
    for c in range(CONVC):
        cols += [wc[:, s * cc + c * 128:s * cc + (c + 1) * 128] for s in (1, 2, 0)]
    parts += [np.concatenate(cols, axis=1), x["w_out"][1]]
    mlp(1)
    wst = np.concatenate([duos(p) for p in parts], axis=0)
    assert wst.shape[0] == 2 * QUADS

    con = np.zeros((128, C_N), np.float32)
    norms = [x["norm_mix"][0], x["norm_mix"][1], x["norm_mlp"][0], x["norm_mlp"][1], x["norm_mem"][0], x["norm_mem"][1]]
    for i, g in enumerate(norms):
        con[:, C_G + 8 * i:C_G + 8 * i + 8] = g.reshape(KC, 128).T
    heads = [x["q_norm_att"][0], x["k_norm_att"][0], x["q_norm_x"][0], x["q_norm_x"][1], x["k_norm_x"][0], x["k_norm_x"][1]]
    for i, g in enumerate(heads):
        con[:, C_HG + i] = np.tile(g, 2)
    con[:, C_CW:C_CW + 18] = x["conv_w"][0].reshape(3, CONVC, 128).transpose(2, 0, 1).reshape(128, 18)
    con[:, C_SINK:C_SINK + 12] = x["sinks"][0][None, :]
    row_kv = (np.arange(128) // ST) % 4
    con[:, C_SROW:C_SROW + 3] = x["sinks"][0].reshape(NKV, GRP)[row_kv]
    p = np.arange(128)
    con[:, C_IDENT:C_IDENT + 128] = np.eye(128)
    con[:, C_ONES:C_ONES + 128] = 1.0
    con[:, C_HEAD:C_HEAD + 128] = p[:, None] // HD == p[None, :] // HD
    con[:, C_SWAP:C_SWAP + 128] = p[:, None] == (p[None, :] ^ (HD // 2))
    key = np.arange(256)[None, :]
    con[:, C_MASKP:C_MASKP + 256] = np.where((key > p[:, None]) & (key <= p[:, None] + 128), 0.0, NEG / SCALE)
    t, key = (p % ST)[:, None], np.arange(132)[None, :]
    con[:, C_MASKS:C_MASKS + 132] = np.where((key > t) & (key <= t + 128), 0.0, NEG / SCALE)
    con[:, C_BLK:C_BLK + SB] = p[:, None] // 16 == np.arange(SB)[None, :]
    con[:, C_ST:C_ST + 96] = x["state_conv"][0].reshape(SB, 2, CONVC, 128).transpose(3, 2, 0, 1).reshape(128, 96)
    con[:, C_EPS] = EPS

    half = HD // 2
    inv = (np.float32(10000.0) ** (-np.arange(half, dtype=np.float32) * np.float32(2.0) / np.float32(HD))).astype(np.float32)
    pos = np.concatenate([np.arange(SEQ), np.tile(PAST + np.arange(ST), SB)]).astype(np.float32)
    ang = (pos[:, None] * inv[None, :]).astype(np.float32)
    cos, sin = np.cos(ang).T, np.sin(ang).T
    rope = np.stack([np.tile(cos, (4, 1)), np.concatenate([-sin, sin, -sin, sin])], axis=1).astype(np.float32)

    kc = x["cache_swa_k"][0].transpose(2, 3, 0, 1).reshape(2, 128, SB, 128).transpose(1, 0, 2, 3)
    vc = x["cache_swa_v"][0].reshape(SB, 128, NKV * HD).transpose(1, 0, 2)
    xk = x["cache_mem_k"].reshape(2, 2, 4, NMEM, 2, 128).transpose(0, 1, 5, 4, 2, 3)
    xv = x["cache_mem_v"].reshape(2, 2, 4, 2, 128, NXH * HD).transpose(0, 1, 4, 3, 2, 5)
    feeds = {
        "xT": feat(np.concatenate([x["x_prompt"][0], x["x_sample"].reshape(NS, D)])),
        "memT": feat(x["mem_prompt"][0]), "wst": wst, "cst": con, "rope": rope,
        "swakT": kc, "swav": vc, "xkT": xk, "xv": xv,
    }
    outs = {
        "yT": (128, KC, NT), "o_kp": (128, 2, 128), "o_vp": (128, 256), "o_cp": (128, CONVC, 2),
        "o_mk": (2, NXH, 64, NMEM), "o_mv": (2, 128, 2, 256), "o_ks": (128, 2, SB, 128),
        "o_vs": (SB, 124, 256), "o_vn": (NS, 256), "o_cs": (128, CONVC, SB, 2),
    }
    nc = bacc.Bacc("TRN2", target_bir_lowering=False, num_devices=1)
    f32 = mybir.dt.float32
    aps, arrays = {}, {}
    for name, a in feeds.items():
        arrays[name] = np.ascontiguousarray(a, dtype=a.dtype)
        aps[name] = nc.dram_tensor(name, arrays[name].shape, f32, kind="ExternalInput").ap()
    for name, shape in outs.items():
        aps[name] = nc.dram_tensor(name, shape, f32, kind="ExternalOutput").ap()
    build_kernel(nc, **aps)
    r = run_bass_kernel_spmd(nc, [arrays], core_ids=[0]).results[0]

    y = r["yT"].transpose(2, 1, 0).reshape(NT, D)
    kp = r["o_kp"].transpose(2, 1, 0).reshape(1, 1, 128, NKV, HD)
    vp = r["o_vp"].reshape(1, 1, 128, NKV, HD)
    cp = r["o_cp"].transpose(2, 1, 0).reshape(1, 1, 2, cc)
    mk = r["o_mk"].transpose(0, 3, 1, 2).reshape(2, 1, NMEM, NXH, HD)
    mv = r["o_mv"].transpose(0, 2, 1, 3).reshape(2, 1, NMEM, NXH, HD)
    ks = r["o_ks"].transpose(2, 3, 1, 0).reshape(1, SB, 128, NKV, HD)
    vs = np.concatenate([r["o_vs"], r["o_vn"].reshape(SB, ST, 256)], axis=1).reshape(1, SB, 128, NKV, HD)
    cs = r["o_cs"].transpose(2, 3, 1, 0).reshape(1, SB, 2, cc)
    return tuple(np.ascontiguousarray(a) for a in
                 (y[:SEQ].reshape(1, SEQ, D), y[SEQ:].reshape(SB, ST, D), kp, vp, cp, mk, mv, ks, vs, cs))
```

```python
from contextlib import ExitStack

import numpy as np

import concourse.bass as bass
from concourse import mybir

D = 1024
SEQ = 512
SB, ST = 8, 4
NS = SB * ST
NT = SEQ + NS
HALF = NT // 2
KC = D // 128
NMEM = 256
HD = 64
NQH, NKV, NXH = 12, 4, 4
GRP = NQH // NKV
CONVC = NQH * HD // 128
FF = 4 * D
GROUPS = FF // D
WROW = 2 * GRP * ST
PAST = 2048
EPS = 1e-6
NEG = -1e30
SCALE = HD ** -0.5
DUO = 256
Q_MEM, Q_ATT, Q_OUT0 = 0, 2, 5
Q_MLP0 = 7
Q_CONV = Q_MLP0 + 4 * GROUPS
Q_OUT1 = Q_CONV + 5
Q_MLP1 = Q_OUT1 + 2
QUADS = Q_MLP1 + 4 * GROUPS
C_G = 0
C_HG = C_G + 48
C_CW = C_HG + 6
C_SINK = C_CW + 18
C_SROW = C_SINK + 12
C_IDENT = C_SROW + 4
C_ONES = C_IDENT + 128
C_HEAD = C_ONES + 128
C_SWAP = C_HEAD + 128
C_MASKP = C_SWAP + 128
C_MASKS = C_MASKP + 256
C_BLK = C_MASKS + 132
C_ST = C_BLK + 2 * SB
C_EPS = C_ST + 96
C_ZERO = C_EPS + 1
C_N = C_ZERO + 1


def build_kernel(nc, xT, memT, wst, cst, rope, swakT, swav, xkT, xv, yT, o_kp, o_vp, o_cp, o_mk, o_mv,
                 o_ks, o_vs, o_vn, o_cs):
    f32, f32r = mybir.dt.float32, mybir.dt.float32r
    ALU, ACT = mybir.AluOpType, mybir.ActivationFunctionType
    base = [(nc.sbuf_base + 63) // 64 * 64]

    def place(name, shape, dt=f32, at=None):
        size = int(np.prod(shape[1:])) * 4
        where = base[0] if at is None else at
        if at is None:
            base[0] += (size + 31) // 32 * 32
            assert base[0] <= nc.sbuf_usable_end, (name, base[0], nc.sbuf_usable_end)
        return nc.alloc_sbuf_tensor_at(name, shape, dt, offset=where), where

    X, _ = place("x_res", [128, KC, NT])
    act_hl, at_act = [], []
    for i in range(2):
        hi, where = place(f"act{i}_hi", [128, KC, NT], f32r)
        lo, _ = place(f"act{i}_lo", [128, KC, NT], f32r)
        act_hl.append((hi, lo))
        at_act.append(where)
    z0, _ = place("z0", [128, 12, NT], at=at_act[1])
    kz, _ = place("kz", [128, NKV, SEQ], at=at_act[1] + 12 * NT * 4)
    z1, _ = place("z1", [128, 2, NT], at=at_act[0])
    at_v = at_act[0] + 2 * NT * 4
    vconv, _ = place("vconv", [128, 2, SEQ + 8], at=at_v)
    at_s = at_v + 2 * (SEQ + 8) * 4
    sconv, _ = place("sconv", [128, CONVC, SB, ST + 2], at=at_s)
    oconv, _ = place("oconv", [128, CONVC, NT], at=at_s + CONVC * SB * (ST + 2) * 4)
    qpad1, _ = place("qpad1", [128, 2, 144 * SB], at=at_s + CONVC * (SB * (ST + 2) + NT) * 4)
    tails, _ = place("tails", [128, CONVC, 2], at=at_s + (CONVC * (SB * (ST + 2) + NT) + 2 * 144 * SB) * 4)
    Zs = [z0, z1]
    NORM_TO = [0, 1, 1, 0]
    stage, _ = place("w_stage", [128, 2, KC, DUO])
    w_hi, _ = place("w_hi", [128, 2, KC, DUO], f32r)
    w_lo, _ = place("w_lo", [128, 2, KC, DUO], f32r)
    rstd, at_rstd = place("rstd", [128, NT])
    ptx, _ = place("ptx", [128, 2, 128], at=at_rstd)
    psq, at_psq = place("psq", [128, NT])
    pacc, _ = place("pacc", [128, NT])
    tmp, at_tmp = place("tmp", [128, 6, NT])
    qwin, _ = place("qwin", [128, 2 * SB, 128 + WROW], at=at_tmp)
    qpad0, _ = place("qpad0", [128, 2, 144 * SB], at=at_tmp)
    pts, _ = place("pts", [128, 2, 4 * 4 * WROW], at=at_tmp + 2 * SB * (128 + WROW) * 4)
    con, _ = place("con", [128, C_N])
    nsink, _ = place("nsink", [128, 16])
    memkz, _ = place("memkz", [128, 2, NXH, NMEM])
    memv, _ = place("memv", [128, 2, 2, NXH * HD])
    vp, at_vp = place("vp", [128, 4, NKV * HD])
    vn, _ = place("vn", [128, NKV * HD])
    ocross, _ = place("ocross", [128, 2, NT], at=at_vp)
    kt, at_kt = place("kt", [128, 2, SB, 132])
    memx, _ = place("memx", [128, KC, NMEM], at=at_kt)
    vb, at_vb = place("vb", [128, SB, NKV * HD])
    kxs = [place(f"kx{i}", [128, 2, 4, NMEM], at=w)[0] for i, w in enumerate((at_kt, at_vb))]
    vxs = [place(f"vx{i}", [128, 2, 4, NXH * HD], at=w)[0] for i, w in enumerate((at_kt, at_vb))]
    sm01, at_sm = place("sm01", [128, 2, 4, 256])
    sm2, _ = place("sm2", [128, 4, 256], at=at_psq)
    sm = [sm01[:, 0], sm01[:, 1], sm2[:, :, :]]
    msq, _ = place("msq", [128, KC, NMEM], at=at_sm)
    pt, at_pt = place("pt", [128, 2, 2, 512])
    cs, _ = place("cs", [128, 2, NT], at=at_pt)
    st, _ = place("st", [128, 3, 5, 4])

    with ExitStack() as ctx:
        def sem(name):
            return ctx.enter_context(nc.semaphore(name))

        zps = [ctx.enter_context(nc.psum_tensor(f"zps{i}", [128, 2, 512], f32)) for i in range(2)]
        tps = ctx.enter_context(nc.psum_tensor("tps", [128, 2, 512], f32))
        ops = ctx.enter_context(nc.psum_tensor("ops", [128, 2, 512], f32))

        w_in = [sem(f"w_in{d}") for d in range(2)]
        w_his = [sem(f"w_his{d}") for d in range(2)]
        w_los = [sem(f"w_los{d}") for d in range(2)]
        z_full = [sem(f"z_full{s}") for s in range(2)]
        z_free = [sem(f"z_free{s}") for s in range(2)]
        ld = {n: sem("ld_" + n) for n in ("con", "con2", "mem0", "mem1", "x", "rope", "kt", "vb", "kx0", "kx1", "vx0", "vx1")}
        m_hi, m_lo = sem("m_hi"), sem("m_lo")
        a_his, a_los = sem("a_his"), sem("a_los")
        sq_acc, pool_ch = sem("sq_acc"), sem("pool_chain")
        s_full, s_sd, s_rstd = sem("s_full"), sem("s_sd"), sem("s_rstd")
        n_sq, n_ms, n_sd, n_out = (sem("n_" + s) for s in ("sq", "ms", "sd", "out"))
        r_sw, r_sin, r_out = sem("r_sw"), sem("r_sin"), sem("r_out")
        mkz_zero, kz_zero, kz_rdy, m_sq = sem("mkz_zero"), sem("kz_zero"), sem("kz_rdy"), sem("m_sq")
        v_t, v_out = sem("v_t"), sem("v_out")
        ch = sem("dve_chain")
        u_sq, u_hi, u_lo = sem("u_sq"), sem("u_hi"), sem("u_lo")
        g_s, g_max, g_sink, g_exp, g_p, g_t, g_pt, g_o, g_ohi, g_olo = (
            sem("g_" + s) for s in ("s", "max", "sink", "exp", "p", "t", "pt", "o", "ohi", "olo"))
        qp_rdy, kt_new, pz = sem("qp_rdy"), sem("kt_new"), sem("pool_zero")
        c_o, c_tail, c_hi, c_lo = (sem("c_" + s) for s in ("o", "tail", "hi", "lo"))
        b_out, ks_out, vs_out, vn_out, stored = (sem(s) for s in ("b_out", "ks_out", "vs_out", "vn_out", "stored"))
        y_out = sem("y_out")

        ident = con[:, C_IDENT:C_IDENT + 128]
        ones = con[:, C_ONES:C_ONES + 128]
        headones = con[:, C_HEAD:C_HEAD + 128]
        swap = con[:, C_SWAP:C_SWAP + 128]
        eps = con[:, C_EPS:C_EPS + 1]

        def gain(norm, k):
            return con[:, C_G + 8 * norm + k:C_G + 8 * norm + k + 1]

        def hgain(i, a=0, b=128):
            return con[a:b, C_HG + i:C_HG + i + 1]

        def tap(j, c):
            return con[:, C_CW + 6 * j + c:C_CW + 6 * j + c + 1]

        def halves(ap2d):
            return ap2d.rearrange("p (h t) -> p h t", h=2)

        def zp(slot, n=HALF):
            return zps[slot][:, :, 0:n]

        def full(eng, q, p):
            eng.wait_ge(z_full[p % 2], q * 2 + (p // 2 + 1))

        def taken(eng, q, p):
            eng.wait_ge(z_free[p % 2], q * 2 + (p // 2 + 1))

        def next_duo(q, p):
            nq, nd = (q, 1) if p == 0 else (q + 1, 0)
            return None if isinstance(nq, int) and nq >= QUADS else (nq, nd)

        NORMS = [("mem", l, c) for l in range(2) for c in range(2)]
        N_ATT = len(NORMS)
        NORMS += [("att", 0, i) for i in range(8)]
        N_QX = [len(NORMS), len(NORMS) + 2]
        NORMS += [("qx", 0, 8), ("qx", 0, 9), ("qx", 1, 0), ("qx", 1, 1)]

        def norm_cols(n):
            return NMEM if NORMS[n][0] == "mem" else NT

        def norm_src(n):
            kind, l, i = NORMS[n]
            return tmp[:, 4, i * 256:(i + 1) * 256] if kind == "mem" else Zs[l][:, i, :]

        def norm_gain(n):
            kind, l, i = NORMS[n]
            return 4 + l if kind == "mem" else (2 + l if kind == "qx" else (1 if i < 2 else 0))

        def norm_panel(n):
            kind, l, i = NORMS[n]
            q0 = {"mem": l, "att": Q_ATT, "qx": Q_ATT if l == 0 else Q_CONV}[kind]
            return q0 + i // 4, i % 4

        GR = [("swa", blk, kv) for blk in range(SEQ // 128) for kv in range(NKV)]
        GR.insert(4, ("ss", 0, 0))
        GR.insert(11, ("sx", 0, 0))
        GR += [("xp", 0, h) for h in range(NXH)]
        G_L1 = len(GR)
        GR += [("sx", 1, 0)] + [("xp", 1, h) for h in range(NXH)]

        def units(j):
            return {"swa": GRP, "xp": 4, "ss": 4, "sx": 1}[GR[j][0]]

        def width(j):
            kind, a, b = GR[j]
            return (128 if a == 0 else 256) if kind == "swa" else (132 if kind == "ss" else 256)

        def first_sink(j):
            kind, a, b = GR[j]
            return {"swa": 3 * b, "ss": NQH}.get(kind)

        def score_banks(j):
            return zps[j % 2] if j < G_L1 else tps

        J_SS = GR.index(("ss", 0, 0))
        J_SX = [GR.index(("sx", l, 0)) for l in range(2)]
        WITH_SX = range(J_SX[0] + 1, J_SX[0] + 5)
        assert [GR[j][2] for j in WITH_SX] == [2, 3, 0, 1]
        PRODUCT, last_use, prod_need = [], [None, None], {}
        for j, (kind, a, b) in enumerate(GR):
            if j == J_SX[0]:
                continue
            pair = kind in ("swa", "xp")
            banks = [(b // 2) % 2] if pair else [0, 1]
            if not pair or b % 2 == 0:
                prod_need[j] = max([last_use[k] for k in banks if last_use[k] is not None], default=None)
            if not pair or b % 2 == 1:
                for k in banks:
                    last_use[k] = len(PRODUCT)
                PRODUCT.append(j)

        XCOL = 512 - 16 * SB
        P_L0 = sum(j < G_L1 for j in PRODUCT)

        def out_of_banks(n):
            return (g_olo, n + 1) if n < P_L0 else (g_ohi, n + 1)

        def product_chunks(n):
            kind, a, b = GR[PRODUCT[n]]
            own = list(range(b // 2 * 3, b // 2 * 3 + 3)) + ([6 + b // 2] if PRODUCT[n] in WITH_SX else [])
            return {"swa": own, "xp": (6 + b // 2,), "ss": range(6), "sx": (6, 7)}[kind]

        def product_parts(n):
            kind, a, b = GR[PRODUCT[n]]
            hp = b // 2
            parts = []
            if kind == "swa":
                parts.append((lambda A, of: A[:, hp * 3:hp * 3 + 3, a * 128:(a + 1) * 128],
                              ops[:, hp, 0:384].rearrange("p (g t) -> p g t", g=3)))
            if kind == "xp":
                parts.append((lambda A, of: A[:, 6 + hp - of, 0:SEQ], ops[:, hp, 0:SEQ]))
            samples = (lambda A, of, r, to: A[r:r + 64, to - of, SEQ:NT].rearrange("p (b t) -> p b t", b=SB))
            heads = {"ss": range(4), "sx": range(4), "swa": range(2 * hp, 2 * hp + 2) if PRODUCT[n] in WITH_SX else []}
            for h in heads.get(kind, []):
                c, r = h // 2, 64 * (h % 2)
                if kind == "ss":
                    rows = ops[r:r + 64, c, 0:SB * WROW].rearrange("p (b k t) -> p b k t", b=SB, t=ST)
                    for g in range(GRP):
                        parts.append((lambda A, of, r=r, to=c * GRP + g: samples(A, of, r, to), rows[:, :, h % 2 * GRP + g, :]))
                else:
                    rows = ops[r:r + 64, c, XCOL:512].rearrange("p (b k t) -> p b k t", b=SB, t=ST)
                    parts.append((lambda A, of, r=r, to=6 + c: samples(A, of, r, to), rows[:, :, h, :]))
            return parts

        O0_READY = [max(n for n in range(P_L0) if k in product_chunks(n)) + 1 for k in range(KC)]
        O1_ORDER = [0, 1, 2, 3, 4, 6, 7, 5]

        def at_s(j):
            return 4 + 3 * (j - G_L1)

        L1 = range(G_L1, len(GR))

        block = ctx.enter_context(nc.Block())

        @block.sync
        def _(sp):
            for d in range(2):
                sp.dma_start(stage[:, d], wst[d]).then_inc(w_in[d], 16)
            with sp.Fori(1, QUADS) as q:
                for d in range(2):
                    sp.wait_ge(w_los[d], q)
                    sp.dma_start(stage[:, d].rearrange("p k n -> p (k n)"),
                                 wst.rearrange("a p k n -> (a p) (k n)")[bass.ds(q * 256 + d * 128, 128), :]
                                 ).then_inc(w_in[d], 16)

        @block.tensor
        def _(pe):
            tfree, ofree = [None], [None]

            def take(cell):
                if cell[0] is not None:
                    pe.wait_ge(*cell[0])

            def panel(q, p, hi, lo, c0=0, c1=NT, ready=None, guard=True, order=range(KC), between=None):
                d, slot, w = p // 2, p % 2, (p % 2) * 128
                if p % 2 == 0:
                    pe.wait_ge(w_los[d], q + 1)
                if guard:
                    pe.wait_ge(z_free[slot], q * 2 + p // 2)
                parts = 2 if c1 - c0 > 512 else 1
                n = (c1 - c0) // parts
                for j, k in enumerate(order):
                    if ready is not None:
                        pe.wait_ge(*ready(j))
                    for i, (w_, r_) in enumerate(((w_hi, hi), (w_hi, lo), (w_lo, hi))):
                        for h in range(parts):
                            mm = pe.matmul(zps[slot][:, h, 0:n], w_[:, d, k, w:w + 128],
                                           r_[:, k, c0 + h * n:c0 + (h + 1) * n],
                                           start=(j == 0 and i == 0), stop=(j == KC - 1 and i == 2))
                    if j == KC - 1:
                        mm.then_inc(z_full[slot], 1)
                    if between is not None:
                        between(j)

            def colsum(n, cols):
                pe.wait_ge(sq_acc, n)
                take(tfree)
                parts = 2 if cols > 512 else 1
                w = cols // parts
                for h in range(parts):
                    mm = pe.matmul(tps[:, h, 0:w], ones, pacc[:, h * w:(h + 1) * w], start=True, stop=True)
                mm.then_inc(s_full, 1)
                tfree[0] = (s_sd, n)

            def headsum(n):
                pe.wait_ge(n_sq, n + 1)
                take(tfree)
                parts = 2 if norm_cols(n) > 512 else 1
                w = norm_cols(n) // parts
                for h in range(parts):
                    mm = pe.matmul(tps[:, h, 0:w], headones, tmp[:, n % 2, h * w:(h + 1) * w], start=True, stop=True)
                mm.then_inc(n_ms, 1)
                tfree[0] = (n_sd, n + 1)

            def swapped(r):
                pe.wait_ge(n_out, N_ATT + r + 1)
                take(ofree)
                for h in range(2):
                    mm = pe.matmul(ops[:, h, 0:HALF], swap, z0[:, r, h * HALF:(h + 1) * HALF], start=True, stop=True)
                mm.then_inc(r_sw, 1)
                ofree[0] = (r_out, r + 1)

            def turn_memv(n):
                l, c = n // 2, n % 2
                taken(pe, Q_MEM + l, 2 + c)
                take(ofree)
                for t in range(2):
                    mm = pe.transpose(ops[:, t, 0:128], tmp[:, 5, c * 256 + t * 128:c * 256 + (t + 1) * 128], ident)
                mm.then_inc(v_t, 1)
                ofree[0] = (v_out, n + 1)

            def turn_v(c):
                taken(pe, Q_ATT + 2, 2 + c)
                take(ofree)
                for t in range(4):
                    pe.transpose(ops[:, 0, t * 128:(t + 1) * 128], z0[:, 10 + c, t * 128:(t + 1) * 128], ident)
                pe.transpose(ops[0:NS, 1, 0:128], z0[:, 10 + c, SEQ:NT], ident).then_inc(v_t, 1)
                ofree[0] = (v_out, 5 + c)

            def scores(j):
                kind, a, b = GR[j]
                s = score_banks(j)
                if j < 2:
                    for p in (2, 3):
                        taken(pe, Q_OUT0 - 1, p)
                if j < G_L1 and j >= 2:
                    pe.wait_ge(g_max, j - 1)
                if j >= G_L1:
                    take(tfree)
                if j < 4:
                    pe.wait_ge(kz_rdy, 2)
                    pe.wait_ge(r_out, 5 if b < 2 else 8)
                for u in range(units(j)):
                    out = s[:, u // 2, (u % 2) * 256:(u % 2) * 256 + width(j)]
                    if kind == "swa":
                        mm = pe.matmul(out, z0[:, 2 + (b // 2) * 3 + u, a * 128:(a + 1) * 128],
                                       kz[:, b, max(a - 1, 0) * 128:(a + 1) * 128], start=True, stop=True)
                    elif kind == "xp":
                        pe.wait_ge(n_out, N_QX[a] + 2)
                        mm = pe.matmul(out, Zs[a][:, (8 if a == 0 else 0) + b // 2, u * 128:(u + 1) * 128],
                                       memkz[:, a, b, :], start=True, stop=True)
                    elif kind == "ss":
                        pe.wait_ge(kt_new, 2)
                        pe.wait_ge(qp_rdy, 1)
                        for bb in range(4):
                            at = u * 4 * (128 + WROW) + bb * 128
                            mm = pe.matmul(out, qwin.rearrange("p k r -> p (k r)")[:, at:at + 128],
                                           kt[:, u // 2, u % 2 * 4 + bb, :], start=(bb == 0), stop=(bb == 3))
                    else:
                        pe.wait_ge(qp_rdy, 2 + a)
                        for hb in range(2):
                            pe.wait_ge(ld[f"kx{hb}"], 16 * (a + 1))
                            for hp in range(2):
                                for bb in range(4):
                                    c = (hb * 4 + bb) * 128
                                    mm = pe.matmul(out, (qpad0, qpad1)[a][:, hp, c:c + 128], kxs[hb][:, hp, bb, :],
                                                   start=(hb == 0 and hp == 0 and bb == 0),
                                                   stop=(hb == 1 and hp == 1 and bb == 3))
                mm.then_inc(g_s, 1)

            def turn_p(j):
                pe.wait_ge(g_p, j + 1)
                take(tfree)
                for u in range(units(j)):
                    for t in range(width(j) // 128):
                        mm = pe.transpose(tps[:, t, u * 128:(u + 1) * 128], sm[j % 3][:, u, t * 128:(t + 1) * 128], ident)
                    if GR[j][0] == "ss":
                        mm = pe.transpose(tps[0:NS, 1, u * 128:(u + 1) * 128], sm[j % 3][:, u, 160:192], ident)
                mm.then_inc(g_t, 1)
                tfree[0] = (g_pt, j + 1)

            def values(j):
                kind, a, b = GR[j]
                if j == J_SX[0]:
                    return
                pe.wait_ge(g_pt, j + 1)
                if j < 2:
                    pe.wait_ge(v_out, 6)
                    take(ofree)
                if prod_need.get(j) is not None:
                    pe.wait_ge(*out_of_banks(prod_need[j]))
                probs = pt[:, j % 2]
                r = 64 * (b % 2)
                if kind == "swa":
                    tiles = [0] if a == 0 else [a - 1, a]
                    for i, t in enumerate(tiles):
                        mm = pe.matmul(ops[r:r + 64, (b // 2) % 2, 0:384], vp[:, t, b * 64:(b + 1) * 64],
                                       probs[:, i, 0:384], start=(i == 0), stop=(i == len(tiles) - 1))
                elif kind == "xp":
                    for i in range(2):
                        mm = pe.matmul(ops[r:r + 64, (b // 2) % 2, 0:SEQ], memv[:, a, i, b * 64:(b + 1) * 64],
                                       probs[:, i, :], start=(i == 0), stop=(i == 1))
                elif kind == "ss":
                    pe.wait_ge(ld["vb"], 16)
                    for hp in range(2):
                        c0 = hp * SB * WROW
                        pe.matmul(ops[:, hp, 0:SB * WROW], vn[0:NS, hp * 128:(hp + 1) * 128],
                                  pts[0:NS, 1, c0:c0 + SB * WROW], start=True, stop=False, skip_group_check=True)
                        for bb in range(SB):
                            mm = pe.matmul(ops[:, hp, bb * WROW:(bb + 1) * WROW], vb[:, bb, hp * 128:(hp + 1) * 128],
                                           pts[:, 0, c0 + bb * WROW:c0 + (bb + 1) * WROW],
                                           start=False, stop=(bb == SB - 1), skip_group_check=True)
                if j in WITH_SX:
                    part = (j - WITH_SX[0]) % 2
                    mm = values_sx(0, range(4 * part, 4 * part + 4), [b // 2])
                if j in PRODUCT:
                    mm.then_inc(g_o, 1)

            def values_sx(l, samples, hps):
                j = J_SX[l]
                probs = (ptx[:, :, :], pt[:, j % 2])[l]
                pe.wait_ge(g_pt, j + 1)
                if l == 1 and samples[0] == 0:
                    pe.wait_ge(*out_of_banks(prod_need[j]))
                for hb in sorted({s_ // 4 for s_ in samples}):
                    pe.wait_ge(ld[f"vx{hb}"], 16 * (l + 1))
                for s_ in samples:
                    for hp in hps:
                        for t in range(2):
                            mm = pe.matmul(ops[:, hp, XCOL + s_ * 16:XCOL + s_ * 16 + 16],
                                           vxs[s_ // 4][:, t, s_ % 4, hp * 128:(hp + 1) * 128],
                                           probs[:, t, s_ * 16:s_ * 16 + 16], start=(t == 0), stop=(t == 1))
                return mm

            def attention_0():
                for j in range(G_L1 + 3):
                    if j < G_L1:
                        scores(j)
                    if j == 0:
                        turn_v(1)
                    if 0 <= j - 2 < G_L1:
                        turn_p(j - 2)
                    if 0 <= j - 3 < G_L1:
                        values(j - 3)

            def out_proj(q0, l, ready, order):
                for m in range(8):
                    if m == 0:
                        panel(q0, 0, *act_hl[l], ready=ready, order=order)
                    else:
                        panel(q0 + m // 4, m % 4, *act_hl[l])

            def mlp_group(q, l, u0, first=None, stat=None):
                for m in range(8):
                    panel(q + m // 4, m % 4, *act_hl[1 - l], ready=first if m == 0 else None)
                    if m == 0 and stat:
                        colsum(stat, NT)
                for m in range(8):
                    panel(q + (2 + m // 4), m % 4, *act_hl[l], ready=(lambda k: (u_lo, u0 + (k + 1))) if m == 0 else None)

            def mlp(q0, l, first, stat):
                mlp_group(q0, l, 32 * l, first, stat)
                with pe.Fori(1, GROUPS) as g:
                    mlp_group(g * 4 + q0, l, g * 8 + 32 * l)

            def normed(n):
                return lambda k: (a_los, 8 * n + k + 1)

            for l in range(2):
                for p in range(4):
                    panel(Q_MEM + l, p, *act_hl[1], l * NMEM, (l + 1) * NMEM,
                          ready=(lambda k: (m_lo, 8 * l + k + 1)) if p == 0 else None, guard=l > 0 or p >= 2)
                    if (l, p) == (0, 0):
                        pe.wait_ge(ld["con2"], 16)
                        colsum(1, NMEM)
                    if p in (1, 2):
                        headsum(2 * l + p - 1)
                    if p == 3:
                        turn_memv(2 * l)
                    if (l, p) == (1, 0):
                        turn_memv(1)
            for i in range(12):
                panel(Q_ATT + i // 4, i % 4, *act_hl[0], ready=normed(0) if i == 0 else None)
                if i == 0:
                    turn_memv(3)
                    colsum(2, NT)
                if 1 <= i <= 10:
                    headsum(N_ATT + i - 1)
                if 2 <= i <= 9:
                    swapped(i - 2)
                if i == 11:
                    turn_v(0)
            attention_0()
            out_proj(Q_OUT0, 0, lambda k: (g_olo, O0_READY[k]), range(KC))
            mlp(Q_MLP0, 0, normed(1), 3)
            def between_sx(k):
                mm = values_sx(1, (k,), (0, 1))
                if k == SB - 1:
                    mm.then_inc(g_o, 1)

            for i in range(20):
                panel(Q_CONV + i // 4, i % 4, *act_hl[1], ready=normed(2) if i == 0 else None,
                      between=between_sx if i == at_s(J_SX[1]) + 4 else None)
                if i == 0:
                    colsum(4, NT)
                if i in (1, 2):
                    headsum(N_QX[1] + i - 1)
                for j in L1:
                    if i == at_s(j) + 2:
                        turn_p(j)
                    if i == at_s(j) + 3 and j != J_SX[1]:
                        values(j)
                for j in L1:
                    if i == at_s(j):
                        scores(j)
            out_proj(Q_OUT1, 1, lambda j: (c_lo, j + 1), O1_ORDER)
            mlp(Q_MLP1, 1, normed(3), 5)

        @block.vector
        def _(dve):
            chained = [0]

            def link(ins):
                chained[0] += 1
                ins.then_inc(ch, 1)
                dve.wait_ge(ch, chained[0])

            def split_lo(q, d):
                dve.wait_ge(w_his[d], q + 1)
                dve.tensor_tensor(w_lo[:, d], stage[:, d], w_hi[:, d].bitcast(f32), ALU.subtract).then_inc(w_los[d], 1)

            def split_next(q, p):
                if p % 2 == 0 and next_duo(q, p):
                    split_lo(*next_duo(q, p))

            def take_scaled(q, p, out, cols=NT):
                full(dve, q, p)
                if cols > 512:
                    ins = dve.tensor_tensor(halves(out), zp(p % 2), halves(rstd[:, :]), ALU.mult)
                else:
                    ins = dve.tensor_tensor(out, zps[p % 2][:, 0, 0:cols], rstd[:, 0:cols], ALU.mult)
                ins.then_inc(z_free[p % 2], 1)

            def inv_rms(n, cols):
                dve.wait_ge(s_sd, n)
                dve.reciprocal(rstd[:, 0:cols], tmp[:, 2, 0:cols]).then_inc(s_rstd, 1)
                dve.wait_ge(s_rstd, n)

            def head_norm(n):
                kind, l, i = NORMS[n]
                cols = norm_cols(n)
                dve.wait_ge(n_sd, n + 1)
                taken(dve, *norm_panel(n))
                link(dve.reciprocal(tmp[:, 3, 0:cols], tmp[:, 2, 0:cols]))
                src = norm_src(n)
                if kind == "mem":
                    dve.wait_ge(mkz_zero, 1)
                    for hf in range(2):
                        r = slice(64 * hf, 64 * hf + 64)
                        ins = dve.scalar_tensor_tensor(out=memkz[r, l, 2 * i + hf, :], in0=src[r],
                                                       scalar=hgain(norm_gain(n), r.start, r.stop),
                                                       in1=tmp[r, 3, 0:cols], op0=ALU.mult, op1=ALU.mult)
                else:
                    ins = dve.scalar_tensor_tensor(out=src, in0=src, scalar=hgain(norm_gain(n)), in1=tmp[:, 3, :],
                                                   op0=ALU.mult, op1=ALU.mult)
                ins.then_inc(n_out, 1)

            def rotary_sin(r):
                dve.wait_ge(r_sw, r + 1)
                if r:
                    dve.wait_ge(r_out, r)
                dve.tensor_tensor(halves(tmp[:, 5, :]), ops[:, :, 0:HALF], halves(cs[:, 1, :]), ALU.mult).then_inc(r_sin, 1)

            def spread_keys(r):
                dve.wait_ge(r_out, r + 1)
                dve.wait_ge(kz_zero, 1)
                for hf in range(2):
                    s = slice(64 * hf, 64 * hf + 64)
                    ins = dve.tensor_copy(kz[s, 2 * r + hf, :], z0[s, r, 0:SEQ])
                ins.then_inc(kz_rdy, 1)

            def turned_v(n):
                dve.wait_ge(v_t, n + 1)
                if n < 4:
                    l, c = n // 2, n % 2
                    dve.tensor_copy(memv[:, l, :, c * 128:(c + 1) * 128], ops[:, :, 0:128]).then_inc(v_out, 1)
                else:
                    c = n - 4
                    link(dve.tensor_copy(vp[:, :, c * 128:(c + 1) * 128], ops[:, 0, :].rearrange("p (t d) -> p t d", t=4)))
                    dve.tensor_copy(vn[0:NS, c * 128:(c + 1) * 128], ops[0:NS, 1, 0:128]).then_inc(v_out, 1)

            def norm_lo(n, k, norm):
                dve.wait_ge(a_his, 8 * n + k + 1)
                hi, lo = act_hl[NORM_TO[n]]
                dve.scalar_tensor_tensor(out=lo[:, k, :], in0=X[:, k, :], scalar=gain(norm, k),
                                         in1=hi[:, k, :].bitcast(f32), op0=ALU.mult, op1=ALU.subtract).then_inc(a_los, 1)

            def residual(q, m):
                p = m % 4
                full(dve, q + m // 4, p)
                dve.wait_ge(z_free[p % 2], (q + m // 4) * 2 + p // 2)
                dve.tensor_tensor(halves(X[:, m, :]), zp(p % 2), halves(X[:, m, :]), ALU.add).then_inc(z_free[p % 2], 1)

            def maxes(j):
                kind, a, b = GR[j]
                n, w = units(j), width(j)
                dve.wait_ge(g_s, j + 1)
                if j >= 3:
                    dve.wait_ge(g_t, j - 2)
                n0 = first_sink(j)
                for u in range(n):
                    s = score_banks(j)[:, u // 2, (u % 2) * 256:(u % 2) * 256 + w]
                    if kind == "swa":
                        mask = con[:, C_MASKP + 256 - w:C_MASKP + 256]
                    elif kind == "ss":
                        mask = con[:, C_MASKS:C_MASKS + 132]
                    else:
                        mask = con[:, C_ZERO:C_ZERO + 1].broadcast_to([128, w])
                    first = 3.0e38 if n0 is None else nsink[:, n0 + u:n0 + u + 1]
                    ins = dve.tensor_tensor_reduce(out=sm[j % 3][:, u, 0:w], in0=s, in1=mask, scale=-SCALE, scalar=first,
                                                   op0=ALU.add, op1=ALU.min, accum_out=st[:, j % 3, 0, u:u + 1])
                ins.then_inc(g_max, 1)
                if n0 is not None:
                    dve.wait_ge(g_max, j + 1)
                    dve.tensor_tensor(st[:, j % 3, 2, 0:n], st[:, j % 3, 0, 0:n], nsink[:, n0:n0 + n],
                                      ALU.subtract).then_inc(g_sink, 1)

            def normalise(j):
                kind = GR[j][0]
                n, w, b = units(j), width(j), j % 3
                dve.wait_ge(g_exp, j + 1)
                total = st[:, b, 1, 0:n]
                if first_sink(j) is not None:
                    link(dve.tensor_tensor(st[:, b, 3, 0:n], total, st[:, b, 2, 0:n], ALU.add))
                    total = st[:, b, 3, 0:n]
                link(dve.reciprocal(st[:, b, 4, 0:n], total))
                for u in range(n):
                    ins = dve.tensor_scalar(sm[b][:, u, 0:w], sm[b][:, u, 0:w], st[:, b, 4, u:u + 1], None, ALU.mult)
                if kind == "ss":
                    link(ins)
                    for u in range(n):
                        own = sm[b][:, u, 128:132].unsqueeze(1).broadcast_to([128, SB, ST])
                        blk = con[:, C_BLK + u % 2 * SB:C_BLK + (u % 2 + 1) * SB].unsqueeze(2).broadcast_to([128, SB, ST])
                        ins = dve.tensor_tensor(sm[b][:, u, 160:192].rearrange("p (b t) -> p b t", b=SB), own, blk, ALU.mult)
                ins.then_inc(g_p, 1)

            def product_lo(n):
                dve.wait_ge(g_ohi, n + 1)
                hi, lo = act_hl[0]
                for dst, src in product_parts(n):
                    ins = dve.tensor_tensor(dst(lo, 0), src, dst(hi, 0).bitcast(f32), ALU.subtract)
                ins.then_inc(g_olo, 1)

            def attention_0():
                for j in range(G_L1 + 4):
                    if j < G_L1:
                        maxes(j)
                    if j == 0:
                        turned_v(5)
                    if 0 <= j - 1 < G_L1:
                        normalise(j - 1)
                    if 0 <= j - 4 < G_L1 and j - 4 in PRODUCT:
                        product_lo(PRODUCT.index(j - 4))

            def out_proj(q0, n, norm):
                for m in range(8):
                    split_next(q0 + m // 4, m % 4)
                    residual(q0, m)
                    taken(dve, q0 + m // 4, m % 4)
                    norm_lo(n, m, norm)

            def hidden_lo(l, u, m):
                dve.wait_ge(u_hi, u + 1)
                hi, lo = act_hl[l]
                dve.tensor_tensor(lo[:, m, :], tmp[:, 3 + m % 2, :], hi[:, m, :].bitcast(f32),
                                  ALU.subtract).then_inc(u_lo, 1)

            def mlp_group(q, l, u0, first=False, stat=None, then=None):
                for m in range(8):
                    split_next(q + m // 4, m % 4)
                    full(dve, q + m // 4, m % 4)
                    if m == 0 and stat:
                        inv_rms(stat, NT)
                    if m >= 2 or not first:
                        dve.wait_ge(u_sq, u0 + (m - 1))
                    dve.scalar_tensor_tensor(out=halves(tmp[:, m % 2, :]), in0=zp(m % 2), scalar=0.0,
                                             in1=halves(rstd[:, :]), op0=ALU.max, op1=ALU.mult).then_inc(z_free[m % 2], 1)
                    if m >= 1:
                        hidden_lo(l, u0 + (m - 1), m - 1)
                hidden_lo(l, u0 + 7, 7)
                for m in range(8):
                    split_next(q + (2 + m // 4), m % 4)
                    residual(q + 2, m)
                    if then:
                        taken(dve, q + 2 + m // 4, m % 4)
                        norm_lo(then[0], m, then[1])

            def mlp(q0, l, stat, then):
                mlp_group(q0, l, 32 * l, first=l == 0, stat=stat)
                with dve.Fori(1, GROUPS - 1) as g:
                    mlp_group(g * 4 + q0, l, g * 8 + 32 * l)
                mlp_group(q0 + 4 * (GROUPS - 1), l, 32 * l + 8 * (GROUPS - 1), then=then)

            def memory_lo(l, k):
                cols = slice(l * NMEM, (l + 1) * NMEM)
                dve.wait_ge(m_hi, 8 * l + k + 1)
                dve.scalar_tensor_tensor(out=act_hl[1][1][:, k, cols], in0=memx[:, k, :], scalar=gain(4 + l, k),
                                         in1=act_hl[1][0][:, k, cols].bitcast(f32), op0=ALU.mult,
                                         op1=ALU.subtract).then_inc(m_lo, 1)

            dve.wait_ge(ld["con"], 16)
            dve.wait_ge(ld["mem0"], 16)
            for k in range(4):
                memory_lo(0, k)
            split_lo(0, 0)
            dve.wait_ge(ld["mem1"], 16)
            for k in range(4, KC):
                memory_lo(0, k)
            dve.wait_ge(m_sq, 2)
            for n in (4, 2):
                link(dve.tensor_tensor(msq[:, 0:n, :], msq[:, 0:n, :], msq[:, n:2 * n, :], ALU.add))
            dve.tensor_tensor(pacc[:, 0:NMEM], msq[:, 0, :], msq[:, 1, :], ALU.add).then_inc(sq_acc, 1)
            link(dve.tensor_scalar(nsink[:, :], con[:, C_SINK:C_SINK + 16], -1.0, None, ALU.mult))
            for k in range(2):
                memory_lo(1, k)
            inv_rms(1, NMEM)
            for k in range(2, KC):
                memory_lo(1, k)
            for l in range(2):
                for p in range(4):
                    q = Q_MEM + l
                    split_next(q, p)
                    take_scaled(q, p, tmp[:, 4 + p // 2, (p % 2) * 256:(p % 2) * 256 + 256], NMEM)
                    if l == 0:
                        for k in (2 * p, 2 * p + 1):
                            norm_lo(0, k, 0)
                    if p in (1, 2):
                        head_norm(2 * l + p - 1)
                    if p == 3:
                        turned_v(2 * l)
                    if (l, p) == (1, 0):
                        turned_v(1)
            dve.wait_ge(ld["rope"], 16)
            dve.wait_ge(ld["con2"], 16)
            for i in range(12):
                q, p = Q_ATT + i // 4, i % 4
                split_next(q, p)
                if i == 0:
                    turned_v(3)
                    inv_rms(2, NT)
                take_scaled(q, p, z0[:, i, :])
                if 2 <= i <= 9:
                    rotary_sin(i - 2)
                if 1 <= i <= 10:
                    head_norm(N_ATT + i - 1)
                if i in (3, 4):
                    spread_keys(i - 3)
                if i == 11:
                    turned_v(4)
            attention_0()
            dve.wait_ge(b_out, 16)
            out_proj(Q_OUT0, 1, 2)
            mlp(Q_MLP0, 0, 3, (2, 1))
            for i in range(20):
                q, p = Q_CONV + i // 4, i % 4
                split_next(q, p)
                if i == 0:
                    inv_rms(4, NT)
                if i < 2:
                    take_scaled(q, p, z1[:, i, :])
                else:
                    c, what = (i - 2) // 3, (i - 2) % 3
                    if what == 0 and c:
                        dve.wait_ge(c_o, c)
                    take_scaled(q, p, tmp[:, 4 if what != 1 else 5, :])
                    taken(dve, q, p)
                    if what == 1:
                        if c < 2:
                            link(dve.memset(vconv[:, c, 0:2], 0.0))
                        if c == 0:
                            link(dve.tensor_copy(sconv[:, :, :, 0:2], con[:, C_ST:C_ST + 96].rearrange(
                                "p (c b t) -> p c b t", c=CONVC, b=SB)))
                        v = vconv[:, c % 2]
                        by_b = (lambda ap: ap.rearrange("p (b t) -> p b t", b=SB))
                        dve.tensor_tensor(v[:, 2:SEQ + 2], tmp[:, 4, 0:SEQ], tmp[:, 5, 0:SEQ], ALU.mult)
                        link(dve.tensor_tensor(sconv[:, c, :, 2:ST + 2], by_b(tmp[:, 4, SEQ:NT]), by_b(tmp[:, 5, SEQ:NT]), ALU.mult))
                        y, ys = tmp[:, 0, 0:SEQ], by_b(tmp[:, 0, SEQ:NT])
                        dve.tensor_copy(tails[:, c, :], v[:, SEQ:SEQ + 2]).then_inc(c_tail, 1)
                        dve.tensor_scalar(y, v[:, 0:SEQ], tap(0, c), None, ALU.mult)
                        link(dve.tensor_scalar(ys, sconv[:, c, :, 0:ST], tap(0, c), None, ALU.mult))
                        for j in (1, 2):
                            dve.scalar_tensor_tensor(out=y, in0=v[:, j:SEQ + j], scalar=tap(j, c), in1=y,
                                                     op0=ALU.mult, op1=ALU.add)
                            link(dve.scalar_tensor_tensor(out=ys, in0=sconv[:, c, :, j:ST + j], scalar=tap(j, c), in1=ys,
                                                          op0=ALU.mult, op1=ALU.add))
                    if what == 2:
                        dve.tensor_tensor(oconv[:, c, :], tmp[:, 4, :], tmp[:, 0, :], ALU.mult).then_inc(c_o, 1)
                if i in (1, 2):
                    head_norm(N_QX[1] + i - 1)
                for j in L1:
                    if i == at_s(j):
                        maxes(j)
                    if i == at_s(j) + 1:
                        normalise(j)
            dve.wait_ge(c_o, CONVC)
            for n, c in enumerate(O1_ORDER):
                dve.wait_ge(c_hi, n + 1)
                src = oconv[:, c, :] if c < 6 else ocross[:, c - 6, :]
                dve.tensor_tensor(act_hl[1][1][:, c, :], src, act_hl[1][0][:, c, :].bitcast(f32), ALU.subtract).then_inc(c_lo, 1)
            dve.wait_ge(b_out, 48)
            out_proj(Q_OUT1, 3, 3)
            mlp(Q_MLP1, 1, 5, None)

        @block.scalar
        def _(act):
            sd_free = [None]

            def copy(out, in_, **kw):
                return act.activation(out, in_, ACT.Copy, **kw)

            def split_hi(q, d, first=False):
                act.wait_ge(w_in[d], q * 16 + 16)
                if not first:
                    act.wait_ge(z_full[1], q * 2 + (d - 1))
                copy(w_hi[:, d], stage[:, d]).then_inc(w_his[d], 1)

            def split_next(q, p):
                if p % 2 == 0 and next_duo(q, p):
                    split_hi(*next_duo(q, p), first=isinstance(q, int) and next_duo(q, p)[0] == 0)

            def root(src, dst, mean_of, sem_in, n, sem_out, free):
                act.wait_ge(sem_in, n)
                if sd_free[0]:
                    act.wait_ge(*sd_free[0])
                act.activation(dst, src, ACT.Sqrt, bias=eps, scale=1.0 / mean_of).then_inc(sem_out, 1)
                sd_free[0] = free

            def root_tokens(n, cols):
                src, dst = (tps[:, :, 0:HALF], halves(tmp[:, 2, :])) if cols > 512 else (tps[:, 0, 0:cols], tmp[:, 2, 0:cols])
                root(src, dst, D, s_full, n, s_sd, (s_rstd, n))

            def root_heads(n):
                cols = norm_cols(n)
                src, dst = (tps[:, :, 0:HALF], halves(tmp[:, 2, :])) if cols > 512 else (tps[:, 0, 0:cols], tmp[:, 2, 0:cols])
                root(src, dst, HD, n_ms, n + 1, n_sd, (n_out, n + 1))

            def square(n):
                taken(act, *norm_panel(n))
                if n >= 2:
                    act.wait_ge(n_ms, n - 1)
                act.activation(tmp[:, n % 2, 0:norm_cols(n)], norm_src(n), ACT.Square).then_inc(n_sq, 1)

            def norm_hi(n, k, norm):
                copy(act_hl[NORM_TO[n]][0][:, k, :], X[:, k, :], scale=gain(norm, k)).then_inc(a_his, 1)

            def exps(j):
                b, n, w = j % 3, units(j), width(j)
                act.wait_ge(g_max, j + 1)
                for u in range(n):
                    ins = act.activation(sm[b][:, u, 0:w], sm[b][:, u, 0:w], ACT.Exp, bias=st[:, b, 0, u:u + 1],
                                         scale=-1.0, accum_out=st[:, b, 1, u:u + 1])
                if first_sink(j) is not None:
                    act.wait_ge(g_sink, sum(first_sink(i) is not None for i in range(j + 1)))
                    ins = act.activation(st[:, b, 2, 0:n], st[:, b, 2, 0:n], ACT.Exp)
                ins.then_inc(g_exp, 1)

            def probs_out(j):
                kind, a, g = GR[j]
                b = j % 2
                act.wait_ge(g_t, j + 1)
                n = units(j) * 128
                if kind == "ss":
                    own = (lambda ap, r: ap.rearrange("p (u r) -> p u r", r=r)[:, :, 0:4 * WROW])
                    copy(own(pts[:, 0, :], 4 * WROW), own(tps[:, 0, :], 128))
                    ins = copy(own(pts[0:NS, 1, :], 4 * WROW), own(tps[0:NS, 1, :], 128))
                elif j == J_SX[0]:
                    ins = copy(ptx[:, :, :], tps[:, :, 0:128])
                elif width(j) == 128:
                    ins = copy(pt[:, b, 0, 0:n], tps[:, 0, 0:n])
                else:
                    ins = copy(pt[:, b, :, 0:n], tps[:, :, 0:n])
                ins.then_inc(g_pt, 1)

            def product_out(n):
                act.wait_ge(g_o, n + 1)
                if n == P_L0:
                    act.wait_ge(vn_out, 32)
                for dst, src in product_parts(n):
                    ins = copy(dst(act_hl[0][0], 0) if n < P_L0 else dst(ocross, 6), src)
                ins.then_inc(g_ohi, 1)

            def attention_0():
                for j in range(G_L1 + 4):
                    if 0 <= j - 2 < G_L1:
                        probs_out(j - 2)
                    if j < G_L1:
                        exps(j)
                    if 0 <= j - 3 < G_L1 and j - 3 in PRODUCT:
                        product_out(PRODUCT.index(j - 3))

            def out_proj(q0, n, norm):
                for m in range(8):
                    split_next(q0 + m // 4, m % 4)
                    taken(act, q0 + m // 4, m % 4)
                    norm_hi(n, m, norm)

            def mlp_group(q, l, u0, first=False, stat=None, then=None, last=False):
                for m in range(8):
                    split_next(q + m // 4, m % 4)
                    if m == 0 and stat:
                        root_tokens(stat, NT)
                    taken(act, q + m // 4, m % 4)
                    if m >= 2 or not first:
                        act.wait_ge(u_lo, u0 + (m - 1))
                    act.activation(tmp[:, 3 + m % 2, :], tmp[:, m % 2, :], ACT.Square).then_inc(u_sq, 1)
                    act.wait_ge(u_sq, u0 + (m + 1))
                    copy(act_hl[l][0][:, m, :], tmp[:, 3 + m % 2, :]).then_inc(u_hi, 1)
                for m in range(8):
                    split_next(q + (2 + m // 4), m % 4)
                    if then is not None:
                        taken(act, q + 2 + m // 4, m % 4)
                        norm_hi(then[0], m, then[1])
                    if last:
                        taken(act, q + 2 + m // 4, m % 4)
                        act.dma_start(yT[:, m, :], X[:, m, :]).then_inc(y_out, 16)

            def mlp(q0, l, stat, then, last):
                mlp_group(q0, l, 32 * l, first=l == 0, stat=stat)
                with act.Fori(1, GROUPS - 1) as g:
                    mlp_group(g * 4 + q0, l, g * 8 + 32 * l)
                mlp_group(q0 + 4 * (GROUPS - 1), l, 32 * l + 8 * (GROUPS - 1), then=then, last=last)

            def memory_hi(l, k):
                copy(act_hl[1][0][:, k, l * NMEM:(l + 1) * NMEM], memx[:, k, :], scale=gain(4 + l, k)).then_inc(m_hi, 1)

            act.dma_start(con[:, 0:C_IDENT], cst[:, 0:C_IDENT]).then_inc(ld["con"], 16)
            for i in range(2):
                act.dma_start(memx[:, 4 * i:4 * i + 4, :], memT[:, 4 * i:4 * i + 4, :]).then_inc(ld[f"mem{i}"], 16)
            act.dma_start(con[:, C_IDENT:C_N], cst[:, C_IDENT:C_N]).then_inc(ld["con2"], 16)
            act.dma_start(X[:, :, :], xT).then_inc(ld["x"], 16)
            act.dma_start(cs[:, :, :], rope).then_inc(ld["rope"], 16)
            act.wait_ge(ld["con"], 16)
            act.wait_ge(ld["mem0"], 16)
            for k in range(4):
                memory_hi(0, k)
            split_hi(0, 0, first=True)
            act.wait_ge(ld["mem1"], 16)
            for k in range(4, KC):
                memory_hi(0, k)
            for i in range(2):
                act.activation(msq[:, 4 * i:4 * i + 4, :], memx[:, 4 * i:4 * i + 4, :], ACT.Square).then_inc(m_sq, 1)
            memory_hi(1, 0)
            memory_hi(1, 1)
            act.wait_ge(ld["con2"], 16)
            root_tokens(1, NMEM)
            for k in range(2, KC):
                memory_hi(1, k)
            act.wait_ge(ld["x"], 16)
            for l in range(2):
                for p in range(4):
                    split_next(Q_MEM + l, p)
                    if l == 0:
                        for k in (2 * p, 2 * p + 1):
                            norm_hi(0, k, 0)
                    if p < 2:
                        square(2 * l + p)
                    if p in (1, 2):
                        root_heads(2 * l + p - 1)
            for i in range(12):
                split_next(Q_ATT + i // 4, i % 4)
                if i == 0:
                    root_tokens(2, NT)
                if i < 10:
                    square(N_ATT + i)
                if 1 <= i <= 10:
                    root_heads(N_ATT + i - 1)
            attention_0()
            act.wait_ge(b_out, 16)
            out_proj(Q_OUT0, 1, 2)
            mlp(Q_MLP0, 0, 3, (2, 1), False)
            for i in range(20):
                split_next(Q_CONV + i // 4, i % 4)
                if i == 0:
                    root_tokens(4, NT)
                if i < 2:
                    square(N_QX[1] + i)
                if i in (1, 2):
                    root_heads(N_QX[1] + i - 1)
                for j in L1:
                    if i == at_s(j):
                        exps(j)
                    if i == at_s(j) + 2:
                        probs_out(j)
                    if i == at_s(j) + (4 if j == J_SX[1] else 3) and j in PRODUCT:
                        product_out(PRODUCT.index(j))
            full(act, Q_OUT1 - 1, 3)
            act.wait_ge(g_ohi, len(PRODUCT))
            for n, c in enumerate(O1_ORDER):
                if c < 6:
                    act.wait_ge(c_o, c + 1)
                copy(act_hl[1][0][:, c, :], oconv[:, c, :] if c < 6 else ocross[:, c - 6, :]).then_inc(c_hi, 1)
            act.wait_ge(b_out, 48)
            out_proj(Q_OUT1, 3, 3)
            mlp(Q_MLP1, 1, 5, None, True)
            act.wait_ge(y_out, 16 * 8)

        @block.gpsimd
        def _(pool):
            n_chain = [0]

            def link(ins):
                n_chain[0] += 1
                ins.then_inc(pool_ch, 1)
                pool.wait_ge(pool_ch, n_chain[0])

            def sum_squares(n, src, cols, before):
                if n > 1:
                    pool.wait_ge(s_full, n - 1)
                for k in range(KC):
                    before(k)
                    x = src[:, k, 0:cols]
                    if k == 0:
                        link(pool.tensor_tensor(pacc[:, 0:cols], x, x, ALU.mult))
                        continue
                    link(pool.tensor_tensor(psq[:, 0:cols], x, x, ALU.mult))
                    ins = pool.tensor_tensor(pacc[:, 0:cols], pacc[:, 0:cols], psq[:, 0:cols], ALU.add)
                    if k < KC - 1:
                        link(ins)
                ins.then_inc(sq_acc, 1)
                pool.wait_ge(sq_acc, n)

            def spread_queries(src, dst):
                for h in range(4):
                    r = slice(64 * (h % 2), 64 * (h % 2) + 64)
                    ins = pool.tensor_copy(dst[r, h // 2, :].rearrange("p (b r) -> p b r", r=144)[:, :, h * 4:h * 4 + 4],
                                           src(h // 2)[r, SEQ:NT].rearrange("p (b t) -> p b t", b=SB))
                ins.then_inc(qp_rdy, 1)

            pool.memset(memkz[:, :, :, :], 0.0).then_inc(mkz_zero, 1)
            pool.wait_ge(ld["x"], 16)
            sum_squares(2, X, NT, lambda k: None)
            pool.dma_start(vb[:, :, :], swav).then_inc(ld["vb"], 16)
            pool.wait_ge(m_lo, 16)
            pool.wait_ge(m_hi, 16)
            pool.wait_ge(m_sq, 2)
            pool.dma_start(kt[:, :, :, 0:128], swakT).then_inc(ld["kt"], 16)
            for p in (2, 3):
                full(pool, Q_ATT - 1, p)
            pool.memset(kz[:, :, :], 0.0).then_inc(kz_zero, 1)
            pool.wait_ge(ld["rope"], 16)
            for r in range(8):
                if r:
                    pool.wait_ge(r_out, r)
                pool.wait_ge(n_out, N_ATT + r + 1)
                link(pool.tensor_tensor(tmp[:, 4, :], z0[:, r, :], cs[:, 0, :], ALU.mult))
                pool.wait_ge(r_sin, r + 1)
                pool.tensor_tensor(z0[:, r, :], tmp[:, 4, :], tmp[:, 5, :], ALU.add).then_inc(r_out, 1)
            pool.wait_ge(r_out, 8)
            pool.wait_ge(ld["kt"], 16)
            for hp in range(2):
                pool.tensor_copy(kt[:, hp, :, 128:132], z0[:, hp, SEQ:NT].rearrange("p (b t) -> p b t", b=SB)).then_inc(kt_new, 1)
            pool.wait_ge(n_out, N_QX[0] + 2)
            pool.memset(qwin[:, :, :], 0.0).then_inc(pz, 1)
            pool.wait_ge(pz, 1)
            for c in range(6):
                for hf in range(2):
                    r, at = slice(64 * hf, 64 * hf + 64), (hf * GRP + c % GRP) * ST
                    ins = pool.tensor_copy(qwin[r, c // GRP * SB:(c // GRP + 1) * SB, at:at + ST],
                                           z0[r, 2 + c, SEQ:NT].rearrange("p (b t) -> p b t", b=SB))
            ins.then_inc(qp_rdy, 1)
            pool.wait_ge(kt_new, 2)
            pool.dma_start(o_ks, kt[:, :, :, ST:132]).then_inc(ks_out, 16)
            pool.dma_start(o_kp, z0[:, 0:2, SEQ - 128:SEQ]).then_inc(b_out, 16)
            pool.wait_ge(ld["vb"], 16)
            pool.dma_start(o_vs.rearrange("b s d -> s b d"), vb[ST:128, :, :]).then_inc(vs_out, 16)
            pool.wait_ge(v_out, 6)
            pool.dma_start(o_vn, vn[0:NS, :]).then_inc(vn_out, 16)
            pool.dma_start(o_vp, vp[:, 3, :]).then_inc(vn_out, 16)
            pool.wait_ge(g_s, J_SS + 1)
            pool.wait_ge(ks_out, 16)
            pool.dma_start(kxs[0][:, :, :, :], xkT[0, 0]).then_inc(ld["kx0"], 16)
            pool.memset(qpad0[:, :, :], 0.0).then_inc(pz, 1)
            pool.wait_ge(pz, 2)
            spread_queries(lambda hp: z0[:, 8 + hp, :], qpad0)
            pool.wait_ge(g_o, PRODUCT.index(J_SS) + 1)
            pool.wait_ge(vs_out, 16)
            pool.dma_start(kxs[1][:, :, :, :], xkT[0, 1]).then_inc(ld["kx1"], 16)
            for l in range(2):
                if l == 1:
                    pool.wait_ge(n_out, N_QX[1] + 2)
                    pool.memset(qpad1[:, :, :], 0.0).then_inc(pz, 1)
                    pool.wait_ge(pz, 3)
                    spread_queries(lambda hp: z1[:, hp, :], qpad1)
                pool.wait_ge(g_s, J_SX[l] + 1)
                for i in range(2):
                    pool.dma_start(vxs[i][:, :, :, :], xv[l, i]).then_inc(ld[f"vx{i}"], 16)
                if l == 0:
                    for i in range(2):
                        for h in range(NXH):
                            r = slice(64 * (h % 2), 64 * (h % 2) + 64)
                            pool.dma_start(o_mk[i, h], memkz[r, i, h, :]).then_inc(stored, 16)
                        pool.dma_start(o_mv[i], memv[:, i, :, :]).then_inc(stored, 16)
                    pool.wait_ge(g_o, PRODUCT.index(WITH_SX[-1]) + 1)
                    for i in range(2):
                        pool.dma_start(kxs[i][:, :, :, :], xkT[1, i]).then_inc(ld[f"kx{i}"], 16)
                    sum_squares(3, X, NT, lambda k: taken(pool, Q_OUT0 + k // 4, k % 4))
                    sum_squares(4, X, NT, lambda k: taken(pool, Q_CONV - 2 + k // 4, k % 4))
            pool.wait_ge(c_tail, CONVC)
            pool.dma_start(o_cp, tails[:, :, :]).then_inc(b_out, 16)
            pool.dma_start(o_cs, sconv[:, :, :, ST:ST + 2]).then_inc(b_out, 16)
            sum_squares(5, X, NT, lambda k: taken(pool, Q_OUT1 + k // 4, k % 4))
            pool.wait_ge(vn_out, 32)
            pool.wait_ge(b_out, 48)
            pool.wait_ge(stored, 16 * 10)


def kernel(**inputs):
    from concourse import bacc
    from concourse.bass_utils import run_bass_kernel_spmd

    x = {k: np.asarray(v) for k, v in inputs.items()}

    def duos(w):
        return w.reshape(KC, 128, -1, DUO).transpose(2, 1, 0, 3)

    def feat(a):
        return a.reshape(-1, KC, 128).transpose(2, 1, 0)

    order = [(2 * hp + hf) * GRP + g for hp in range(2) for g in range(GRP) for hf in range(2)]
    qcols = np.concatenate([np.arange(h * HD, (h + 1) * HD) for h in order])
    c0, c1, c2 = NQH * HD, (NQH + NKV) * HD, (NQH + 2 * NKV) * HD
    wa = x["w_in_att"][0]
    parts = [x["w_mem_kv"][0], x["w_mem_kv"][1],
             np.concatenate([wa[:, c0:c1], wa[:, qcols], wa[:, c2:], wa[:, c1:c2]], axis=1),
             np.concatenate([x["w_out"][0][qcols], x["w_out"][0][c0:]], axis=0)]

    def mlp(l):
        for g in range(GROUPS):
            parts.append(x["w_up"][l][:, g * D:(g + 1) * D])
            parts.append(x["w_down"][l][g * D:(g + 1) * D])

    mlp(0)
    wc = x["w_in_conv"][0]
    cc = CONVC * 128
    cols = [wc[:, 3 * cc:]]
    for c in range(CONVC):
        cols += [wc[:, s * cc + c * 128:s * cc + (c + 1) * 128] for s in (1, 2, 0)]
    parts += [np.concatenate(cols, axis=1), x["w_out"][1]]
    mlp(1)
    wst = np.concatenate([duos(p) for p in parts], axis=0)
    assert wst.shape[0] == 2 * QUADS

    con = np.zeros((128, C_N), np.float32)
    norms = [x["norm_mix"][0], x["norm_mix"][1], x["norm_mlp"][0], x["norm_mlp"][1], x["norm_mem"][0], x["norm_mem"][1]]
    for i, g in enumerate(norms):
        con[:, C_G + 8 * i:C_G + 8 * i + 8] = g.reshape(KC, 128).T
    heads = [x["q_norm_att"][0], x["k_norm_att"][0], x["q_norm_x"][0], x["q_norm_x"][1], x["k_norm_x"][0], x["k_norm_x"][1]]
    for i, g in enumerate(heads):
        con[:, C_HG + i] = np.tile(g, 2)
    con[:, C_CW:C_CW + 18] = x["conv_w"][0].reshape(3, CONVC, 128).transpose(2, 0, 1).reshape(128, 18)
    con[:, C_SINK:C_SINK + 12] = x["sinks"][0][None, :]
    row = np.arange(128) % WROW // ST
    for u in range(4):
        con[:, C_SROW + u] = x["sinks"][0].reshape(NKV, GRP)[u // 2 * 2 + row // GRP, row % GRP]
    p = np.arange(128)
    con[:, C_IDENT:C_IDENT + 128] = np.eye(128)
    con[:, C_ONES:C_ONES + 128] = 1.0
    con[:, C_HEAD:C_HEAD + 128] = p[:, None] // HD == p[None, :] // HD
    con[:, C_SWAP:C_SWAP + 128] = p[:, None] == (p[None, :] ^ (HD // 2))
    key = np.arange(256)[None, :]
    con[:, C_MASKP:C_MASKP + 256] = np.where((key > p[:, None]) & (key <= p[:, None] + 128), 0.0, NEG / SCALE)
    t, key = (p % ST)[:, None], np.arange(132)[None, :]
    con[:, C_MASKS:C_MASKS + 132] = np.where((key > t) & (key <= t + 128), 0.0, NEG / SCALE)
    for half in range(2):
        con[:, C_BLK + half * SB:C_BLK + (half + 1) * SB] = p[:, None] // WROW + 4 * half == np.arange(SB)[None, :]
    con[:, C_ST:C_ST + 96] = x["state_conv"][0].reshape(SB, 2, CONVC, 128).transpose(3, 2, 0, 1).reshape(128, 96)
    con[:, C_EPS] = EPS

    half = HD // 2
    inv = (np.float32(10000.0) ** (-np.arange(half, dtype=np.float32) * np.float32(2.0) / np.float32(HD))).astype(np.float32)
    pos = np.concatenate([np.arange(SEQ), np.tile(PAST + np.arange(ST), SB)]).astype(np.float32)
    ang = (pos[:, None] * inv[None, :]).astype(np.float32)
    cos, sin = np.cos(ang).T, np.sin(ang).T
    rope = np.stack([np.tile(cos, (4, 1)), np.concatenate([-sin, sin, -sin, sin])], axis=1).astype(np.float32)

    kc = x["cache_swa_k"][0].transpose(2, 3, 0, 1).reshape(2, 128, SB, 128).transpose(1, 0, 2, 3)
    vc = x["cache_swa_v"][0].reshape(SB, 128, NKV * HD).transpose(1, 0, 2)
    xk = x["cache_mem_k"].reshape(2, 2, 4, NMEM, 2, 128).transpose(0, 1, 5, 4, 2, 3)
    xv = x["cache_mem_v"].reshape(2, 2, 4, 2, 128, NXH * HD).transpose(0, 1, 4, 3, 2, 5)
    feeds = {
        "xT": feat(np.concatenate([x["x_prompt"][0], x["x_sample"].reshape(NS, D)])),
        "memT": feat(x["mem_prompt"][0]), "wst": wst, "cst": con, "rope": rope,
        "swakT": kc, "swav": vc, "xkT": xk, "xv": xv,
    }
    outs = {
        "yT": (128, KC, NT), "o_kp": (128, 2, 128), "o_vp": (128, 256), "o_cp": (128, CONVC, 2),
        "o_mk": (2, NXH, 64, NMEM), "o_mv": (2, 128, 2, 256), "o_ks": (128, 2, SB, 128),
        "o_vs": (SB, 124, 256), "o_vn": (NS, 256), "o_cs": (128, CONVC, SB, 2),
    }
    nc = bacc.Bacc("TRN2", target_bir_lowering=False, num_devices=1)
    f32 = mybir.dt.float32
    aps, arrays = {}, {}
    for name, a in feeds.items():
        arrays[name] = np.ascontiguousarray(a, dtype=a.dtype)
        aps[name] = nc.dram_tensor(name, arrays[name].shape, f32, kind="ExternalInput").ap()
    for name, shape in outs.items():
        aps[name] = nc.dram_tensor(name, shape, f32, kind="ExternalOutput").ap()
    build_kernel(nc, **aps)
    r = run_bass_kernel_spmd(nc, [arrays], core_ids=[0]).results[0]

    y = r["yT"].transpose(2, 1, 0).reshape(NT, D)
    kp = r["o_kp"].transpose(2, 1, 0).reshape(1, 1, 128, NKV, HD)
    vp = r["o_vp"].reshape(1, 1, 128, NKV, HD)
    cp = r["o_cp"].transpose(2, 1, 0).reshape(1, 1, 2, cc)
    mk = r["o_mk"].transpose(0, 3, 1, 2).reshape(2, 1, NMEM, NXH, HD)
    mv = r["o_mv"].transpose(0, 2, 1, 3).reshape(2, 1, NMEM, NXH, HD)
    ks = r["o_ks"].transpose(2, 3, 1, 0).reshape(1, SB, 128, NKV, HD)
    vs = np.concatenate([r["o_vs"], r["o_vn"].reshape(SB, ST, 256)], axis=1).reshape(1, SB, 128, NKV, HD)
    cs = r["o_cs"].transpose(2, 3, 1, 0).reshape(1, SB, 2, cc)
    return tuple(np.ascontiguousarray(a) for a in
                 (y[:SEQ].reshape(1, SEQ, D), y[SEQ:].reshape(SB, ST, D), kp, vp, cp, mk, mv, ks, vs, cs))
```

```python
from contextlib import ExitStack

import numpy as np

import concourse.bass as bass
from concourse import mybir

D = 1024
SEQ = 512
SB, ST = 8, 4
NS = SB * ST
NT = SEQ + NS
HALF = NT // 2
KC = D // 128
NMEM = 256
HD = 64
NQH, NKV, NXH = 12, 4, 4
GRP = NQH // NKV
CONVC = NQH * HD // 128
FF = 4 * D
GROUPS = FF // D
WROW = 2 * GRP * ST
PAST = 2048
EPS = 1e-6
NEG = -1e30
SCALE = HD ** -0.5
DUO = 256
Q_MEM, Q_ATT, Q_OUT0 = 0, 2, 5
Q_MLP0 = 7
Q_CONV = Q_MLP0 + 4 * GROUPS
Q_OUT1 = Q_CONV + 5
Q_MLP1 = Q_OUT1 + 2
QUADS = Q_MLP1 + 4 * GROUPS
C_G = 0
C_HG = C_G + 48
C_CW = C_HG + 6
C_SINK = C_CW + 18
C_SROW = C_SINK + 12
C_IDENT = C_SROW + 4
C_ONES = C_IDENT + 128
C_HEAD = C_ONES + 128
C_MASKP = C_HEAD + 128
C_MASKS = C_MASKP + 256
C_BLK = C_MASKS + 132
C_ST = C_BLK + 2 * SB
C_EPS = C_ST + 96
C_ZERO = C_EPS + 1
C_N = C_ZERO + 1


def build_kernel(nc, xT, memT, wst, cst, rope, swakT, swav, xkT, xv, yT, o_kp, o_vp, o_cp, o_mk, o_mv,
                 o_ks, o_vs, o_vn, o_cs):
    f32, f32r = mybir.dt.float32, mybir.dt.float32r
    ALU, ACT = mybir.AluOpType, mybir.ActivationFunctionType
    base = [(nc.sbuf_base + 63) // 64 * 64]

    def place(name, shape, dt=f32, at=None):
        size = int(np.prod(shape[1:])) * 4
        where = base[0] if at is None else at
        if at is None:
            base[0] += (size + 31) // 32 * 32
            assert base[0] <= nc.sbuf_usable_end, (name, base[0], nc.sbuf_usable_end)
        return nc.alloc_sbuf_tensor_at(name, shape, dt, offset=where), where

    X, _ = place("x_res", [128, KC, NT])
    act_hl, at_act = [], []
    for i in range(2):
        hi, where = place(f"act{i}_hi", [128, KC, NT], f32r)
        lo, _ = place(f"act{i}_lo", [128, KC, NT], f32r)
        act_hl.append((hi, lo))
        at_act.append(where)
    z0, _ = place("z0", [128, 12, NT], at=at_act[1])
    kz, _ = place("kz", [128, NKV, SEQ], at=at_act[1] + 12 * NT * 4)
    z1, _ = place("z1", [128, 2, NT], at=at_act[0])
    at_v = at_act[0] + 2 * NT * 4
    vconv, _ = place("vconv", [128, 2, SEQ + 8], at=at_v)
    at_s = at_v + 2 * (SEQ + 8) * 4
    sconv, _ = place("sconv", [128, CONVC, SB, ST + 2], at=at_s)
    oconv, _ = place("oconv", [128, CONVC, NT], at=at_s + CONVC * SB * (ST + 2) * 4)
    qpad1, _ = place("qpad1", [128, 2, 144 * SB], at=at_s + CONVC * (SB * (ST + 2) + NT) * 4)
    tails, _ = place("tails", [128, CONVC, 2], at=at_s + (CONVC * (SB * (ST + 2) + NT) + 2 * 144 * SB) * 4)
    Zs = [z0, z1]
    NORM_TO = [0, 1, 1, 0]
    stage, _ = place("w_stage", [128, 2, KC, DUO])
    w_hi, _ = place("w_hi", [128, 2, KC, DUO], f32r)
    w_lo, _ = place("w_lo", [128, 2, KC, DUO], f32r)
    rstd, at_rstd = place("rstd", [128, NT])
    ptx, _ = place("ptx", [128, 2, 128], at=at_rstd)
    psq, at_psq = place("psq", [128, NT])
    pacc, _ = place("pacc", [128, NT])
    tmp, at_tmp = place("tmp", [128, 6, NT])
    qwin, _ = place("qwin", [128, 2 * SB, 128 + WROW], at=at_tmp)
    qpad0, _ = place("qpad0", [128, 2, 144 * SB], at=at_tmp)
    pts, _ = place("pts", [128, 2, 4 * 4 * WROW], at=at_tmp + 2 * SB * (128 + WROW) * 4)
    con, _ = place("con", [128, C_N])
    nsink, _ = place("nsink", [128, 16])
    memkz, _ = place("memkz", [128, 2, NXH, NMEM])
    memv, _ = place("memv", [128, 2, 2, NXH * HD])
    vp, at_vp = place("vp", [128, 4, NKV * HD])
    vn, _ = place("vn", [128, NKV * HD])
    ocross, _ = place("ocross", [128, 2, NT], at=at_vp)
    kt, at_kt = place("kt", [128, 2, SB, 132])
    memx, _ = place("memx", [128, KC, NMEM], at=at_kt)
    vb, at_vb = place("vb", [128, SB, NKV * HD])
    kxs = [place(f"kx{i}", [128, 2, 4, NMEM], at=w)[0] for i, w in enumerate((at_kt, at_vb))]
    vxs = [place(f"vx{i}", [128, 2, 4, NXH * HD], at=w)[0] for i, w in enumerate((at_kt, at_vb))]
    sm01, at_sm = place("sm01", [128, 2, 4, 256])
    sm2, _ = place("sm2", [128, 4, 256], at=at_psq)
    sm = [sm01[:, 0], sm01[:, 1], sm2[:, :, :]]
    msq, _ = place("msq", [128, KC, NMEM], at=at_sm)
    pt, at_pt = place("pt", [128, 2, 2, 512])
    cs, _ = place("cs", [128, 2, NT], at=at_pt)
    st, _ = place("st", [128, 3, 5, 4])

    with ExitStack() as ctx:
        def sem(name):
            return ctx.enter_context(nc.semaphore(name))

        zps = [ctx.enter_context(nc.psum_tensor(f"zps{i}", [128, 2, 512], f32)) for i in range(2)]
        tps = ctx.enter_context(nc.psum_tensor("tps", [128, 2, 512], f32))
        ops = ctx.enter_context(nc.psum_tensor("ops", [128, 2, 512], f32))

        w_in = [sem(f"w_in{d}") for d in range(2)]
        w_his = [sem(f"w_his{d}") for d in range(2)]
        w_his_half, w_los_half = sem("w_his_half"), sem("w_los_half")
        w_los = [sem(f"w_los{d}") for d in range(2)]
        z_full = [sem(f"z_full{s}") for s in range(2)]
        z_free = [sem(f"z_free{s}") for s in range(2)]
        ld = {n: sem("ld_" + n) for n in ("con", "con2", "mem0", "mem1", "x", "rope", "kt", "vb", "kx0", "kx1", "vx0", "vx1")}
        m_hi, m_full, m_los = sem("m_hi"), sem("m_full"), [sem(f"m_lo{l}") for l in range(2)]
        a_his, a_los = sem("a_his"), sem("a_los")
        sq_acc, pool_ch = sem("sq_acc"), sem("pool_chain")
        s_full, s_sd, s_rstd = sem("s_full"), sem("s_sd"), sem("s_rstd")
        n_sq, n_ms, n_sd, n_out = (sem("n_" + s) for s in ("sq", "ms", "sd", "out"))
        r_sw, r_out = [sem(f"r_sw{i}") for i in range(2)], sem("r_out")
        zeroed, kz_rdy = sem("zeroed"), sem("kz_rdy")
        v_t, v_out = sem("v_t"), sem("v_out")
        ch = sem("dve_chain")
        u_sq, u_hi, u_lo = sem("u_sq"), sem("u_hi"), sem("u_lo")
        g_s, g_max, g_sink, g_exp, g_p, g_t, g_pt, g_o, g_ohi, g_olo = (
            sem("g_" + s) for s in ("s", "max", "sink", "exp", "p", "t", "pt", "o", "ohi", "olo"))
        qp_rdy, kt_new = sem("qp_rdy"), sem("kt_new")
        c_o, c_tail, c_read, c_hi, c_lo = (sem("c_" + s) for s in ("o", "tail", "read", "hi", "lo"))
        b_out, win_out, vn_out, stored = (sem(s) for s in ("b_out", "win_out", "vn_out", "stored"))
        y_out = sem("y_out")

        ident = con[:, C_IDENT:C_IDENT + 128]
        ones = con[:, C_ONES:C_ONES + 128]
        headones = con[:, C_HEAD:C_HEAD + 128]
        eps = con[:, C_EPS:C_EPS + 1]

        def gain(norm, k):
            return con[:, C_G + 8 * norm + k:C_G + 8 * norm + k + 1]

        def hgain(i, a=0, b=128):
            return con[a:b, C_HG + i:C_HG + i + 1]

        def tap(j, c):
            return con[:, C_CW + 6 * j + c:C_CW + 6 * j + c + 1]

        def halves(ap2d):
            return ap2d.rearrange("p (h t) -> p h t", h=2)

        def zp(slot, n=HALF):
            return zps[slot][:, :, 0:n]

        def full(eng, q, p):
            eng.wait_ge(z_full[p % 2], q * 2 + (p // 2 + 1))

        def taken(eng, q, p):
            eng.wait_ge(z_free[p % 2], q * 2 + (p // 2 + 1))

        def next_duo(q, p):
            nq, nd = (q, 1) if p == 0 else (q + 1, 0)
            return None if isinstance(nq, int) and nq >= QUADS else (nq, nd)

        NORMS = [("mem", l, c) for l in range(2) for c in range(2)]
        N_ATT = len(NORMS)
        NORMS += [("att", 0, i) for i in range(8)]
        N_QX = [len(NORMS), len(NORMS) + 2]
        NORMS += [("qx", 0, 8), ("qx", 0, 9), ("qx", 1, 0), ("qx", 1, 1)]

        def norm_cols(n):
            return NMEM if NORMS[n][0] == "mem" else NT

        def norm_src(n):
            kind, l, i = NORMS[n]
            return tmp[:, 4, i * 256:(i + 1) * 256] if kind == "mem" else Zs[l][:, i, :]

        def norm_gain(n):
            kind, l, i = NORMS[n]
            return 4 + l if kind == "mem" else (2 + l if kind == "qx" else (1 if i < 2 else 0))

        def norm_panel(n):
            kind, l, i = NORMS[n]
            q0 = {"mem": l, "att": Q_ATT, "qx": Q_ATT if l == 0 else Q_CONV}[kind]
            return q0 + i // 4, i % 4

        GR = [("swa", blk, kv) for blk in range(SEQ // 128) for kv in ((2, 3, 0, 1) if blk == 1 else range(NKV))]
        GR.insert(4, ("ss", 0, 0))
        GR.insert(13, ("sx", 0, 0))
        GR += [("xp", 0, h) for h in range(NXH)]
        G_L1 = len(GR)
        GR += [("sx", 1, 0)] + [("xp", 1, h) for h in range(NXH)]

        def units(j):
            return {"swa": GRP, "xp": 4, "ss": 4, "sx": 1}[GR[j][0]]

        def width(j):
            kind, a, b = GR[j]
            return (128 if a == 0 else 256) if kind == "swa" else (132 if kind == "ss" else 256)

        def first_sink(j):
            kind, a, b = GR[j]
            return {"swa": 3 * b, "ss": NQH}.get(kind)

        def score_cols(j, u):
            if j < 2:
                return ops[:, j, u * 128:(u + 1) * 128]
            s = zps[j % 2] if j < G_L1 else tps
            return s[:, u // 2, (u % 2) * 256:(u % 2) * 256 + width(j)]

        J_SS = GR.index(("ss", 0, 0))
        J_SX = [GR.index(("sx", l, 0)) for l in range(2)]
        WITH_SX = range(J_SX[0] + 1, J_SX[0] + 5)
        assert [GR[j][2] for j in WITH_SX] == [0, 1, 2, 3]
        assert [GR[j][2] for j in (J_SS - 1, J_SS + 1, J_SS + 4, J_SS + 5)] == [3, 2, 1, 0]
        PRODUCT, last_use, prod_need = [], [None, None], {}

        def add_product(key, banks, first=True, last=True):
            if first:
                prod_need[key] = max([last_use[k] for k in banks if last_use[k] is not None], default=None)
            if last:
                for k in banks:
                    last_use[k] = len(PRODUCT)
                PRODUCT.append(key)

        for j, (kind, a, b) in enumerate(GR):
            if kind in ("swa", "xp"):
                add_product(GR[j], [b // 2], b % 2 == 0, b % 2 == 1)
            if j in (J_SS, J_SS + 4):
                hp = (j - J_SS) // 4
                add_product(("ss", 0, hp), [hp])
            if j == J_SX[1]:
                add_product(GR[j], [0, 1])

        def products_at(j):
            keys = [GR[j]] if GR[j][0] in ("swa", "xp") and GR[j][2] % 2 == 1 or j == J_SX[1] else []
            if j in (J_SS, J_SS + 4):
                keys.append(("ss", 0, (j - J_SS) // 4))
            return [PRODUCT.index(key) for key in keys]

        XCOL = 512 - 16 * SB
        P_L0 = len(PRODUCT) - 3

        def out_of_banks(n):
            return (g_olo, n + 1) if n < P_L0 else (g_ohi, n + 1)

        def with_sx(n):
            return PRODUCT[n] in [GR[j] for j in WITH_SX]

        def product_chunks(n):
            kind, a, b = PRODUCT[n]
            own = list(range(b // 2 * 3, b // 2 * 3 + 3)) + ([6 + b // 2] if with_sx(n) else [])
            return {"swa": own, "xp": (6 + b // 2,), "ss": range(b * 3, b * 3 + 3), "sx": (6, 7)}[kind]

        def product_parts(n):
            kind, a, b = PRODUCT[n]
            hp = b // 2
            parts = []
            if kind == "swa":
                parts.append((lambda A, of: A[:, hp * 3:hp * 3 + 3, a * 128:(a + 1) * 128],
                              ops[:, hp, 0:384].rearrange("p (g t) -> p g t", g=3)))
            if kind == "xp":
                parts.append((lambda A, of: A[:, 6 + hp - of, 0:SEQ], ops[:, hp, 0:SEQ]))
            samples = (lambda A, of, r, to: A[r:r + 64, to - of, SEQ:NT].rearrange("p (b t) -> p b t", b=SB))
            heads = {"ss": (2 * b, 2 * b + 1), "sx": range(4), "swa": (2 * hp, 2 * hp + 1) if with_sx(n) else ()}
            for h in heads.get(kind, []):
                c, r = h // 2, 64 * (h % 2)
                if kind == "ss":
                    rows = ops[r:r + 64, c, 0:SB * WROW].rearrange("p (b f g t) -> p f g b t", b=SB, f=2, t=ST)
                    parts.append((lambda A, of, r=r, c=c: A[r:r + 64, c * GRP:(c + 1) * GRP, SEQ:NT].rearrange(
                        "p g (b t) -> p g b t", b=SB), rows[:, h % 2]))
                else:
                    rows = ops[r:r + 64, c, XCOL:512].rearrange("p (b k t) -> p b k t", b=SB, t=ST)
                    parts.append((lambda A, of, r=r, to=6 + c: samples(A, of, r, to), rows[:, :, h, :]))
            return parts

        O0_READY = [max(n for n in range(P_L0) if k in product_chunks(n)) + 1 for k in range(KC)]
        O1_ORDER = [0, 1, 2, 3, 4, 6, 7, 5]

        def at_s(j):
            return 4 + 3 * (j - G_L1)

        L1 = range(G_L1, len(GR))
        EARLY = 3

        block = ctx.enter_context(nc.Block())

        @block.sync
        def _(sp):
            for i in range(2):
                sp.dma_start(memx[:, 4 * i:4 * i + 4, :], memT[:, 4 * i:4 * i + 4, :]).then_inc(ld[f"mem{i}"], 16)
            for d in range(2):
                sp.dma_start(stage[:, d], wst[d]).then_inc(w_in[d], 16)
            with sp.Fori(1, QUADS) as q:
                for d in range(2):
                    sp.wait_ge(w_los[d], q)
                    sp.dma_start(stage[:, d].rearrange("p k n -> p (k n)"),
                                 wst.rearrange("a p k n -> (a p) (k n)")[bass.ds(q * 256 + d * 128, 128), :]
                                 ).then_inc(w_in[d], 16)

        @block.tensor
        def _(pe):
            tfree, ofree = [None], [None]

            def take(cell):
                if cell[0] is not None:
                    pe.wait_ge(*cell[0])

            def panel(q, p, hi, lo, c0=0, c1=NT, ready=None, guard=True, order=range(KC), between=None):
                d, slot, w = p // 2, p % 2, (p % 2) * 128
                if not guard and p == 0:
                    pe.wait_ge(w_los_half, 1)
                elif p % 2 == 0 or not guard:
                    pe.wait_ge(w_los[d], q + 1)
                if guard:
                    pe.wait_ge(z_free[slot], q * 2 + p // 2)
                parts = 2 if c1 - c0 > 512 else 1
                n = (c1 - c0) // parts
                for j, k in enumerate(order):
                    if ready is not None:
                        pe.wait_ge(*ready(j))
                    for i, (w_, r_) in enumerate(((w_hi, hi), (w_hi, lo), (w_lo, hi))):
                        for h in range(parts):
                            mm = pe.matmul(zps[slot][:, h, 0:n], w_[:, d, k, w:w + 128],
                                           r_[:, k, c0 + h * n:c0 + (h + 1) * n],
                                           start=(j == 0 and i == 0), stop=(j == KC - 1 and i == 2))
                    if j == KC - 1:
                        mm.then_inc(z_full[slot], 1)
                    if between is not None:
                        between(j, mm)

            def colsum(n, cols):
                pe.wait_ge(sq_acc, n)
                take(tfree)
                parts = 2 if cols > 512 else 1
                w = cols // parts
                for h in range(parts):
                    mm = pe.matmul(tps[:, h, 0:w], ones, pacc[:, h * w:(h + 1) * w], start=True, stop=True)
                mm.then_inc(s_full, 1)
                tfree[0] = (s_sd, n)

            def headsum(n):
                pe.wait_ge(n_sq, n + 1)
                take(tfree)
                parts = 2 if norm_cols(n) > 512 else 1
                w = norm_cols(n) // parts
                for h in range(parts):
                    mm = pe.matmul(tps[:, h, 0:w], headones, tmp[:, n % 2, h * w:(h + 1) * w], start=True, stop=True)
                mm.then_inc(n_ms, 1)
                tfree[0] = (n_sd, n + 1)

            def turn_memv(n):
                l, c = n // 2, n % 2
                taken(pe, Q_MEM + l, 2 + c)
                take(ofree)
                for t in range(2):
                    mm = pe.transpose(ops[:, t, 0:128], tmp[:, 5, c * 256 + t * 128:c * 256 + (t + 1) * 128], ident)
                mm.then_inc(v_t, 1)
                ofree[0] = (v_out, n + 1)

            def turn_v(c):
                taken(pe, Q_ATT + 2, 2 + c)
                take(ofree)
                for t in range(4):
                    pe.transpose(ops[:, 0, t * 128:(t + 1) * 128], z0[:, 10 + c, t * 128:(t + 1) * 128], ident)
                pe.transpose(ops[0:NS, 1, 0:128], z0[:, 10 + c, SEQ:NT], ident).then_inc(v_t, 1)
                ofree[0] = (v_out, 5 + c)

            def scores(j):
                kind, a, b = GR[j]
                if j == 0:
                    take(ofree)
                    ofree[0] = (g_max, 2)
                if j in (2, 3):
                    for p in (2, 3):
                        taken(pe, Q_OUT0 - 1, p)
                if 4 <= j < G_L1:
                    pe.wait_ge(g_max, j - 1)
                if j >= G_L1:
                    take(tfree)
                if j < 4:
                    pe.wait_ge(kz_rdy, 2)
                    pe.wait_ge(r_out, 5 if b < 2 else 8)
                for u in range(units(j)):
                    out = score_cols(j, u)
                    if kind == "swa":
                        mm = pe.matmul(out, z0[:, 2 + (b // 2) * 3 + u, a * 128:(a + 1) * 128],
                                       kz[:, b, max(a - 1, 0) * 128:(a + 1) * 128], start=True, stop=True)
                    elif kind == "xp":
                        pe.wait_ge(n_out, N_QX[a] + 2)
                        mm = pe.matmul(out, Zs[a][:, (8 if a == 0 else 0) + b // 2, u * 128:(u + 1) * 128],
                                       memkz[:, a, b, :], start=True, stop=True)
                    elif kind == "ss":
                        pe.wait_ge(kt_new, 2)
                        pe.wait_ge(qp_rdy, 1)
                        for bb in range(4):
                            at = u * 4 * (128 + WROW) + bb * 128
                            mm = pe.matmul(out, qwin.rearrange("p k r -> p (k r)")[:, at:at + 128],
                                           kt[:, u // 2, u % 2 * 4 + bb, :], start=(bb == 0), stop=(bb == 3))
                    else:
                        pe.wait_ge(qp_rdy, 2 + a)
                        for hb in range(2):
                            pe.wait_ge(ld[f"kx{hb}"], 16 * (a + 1))
                            for hp in range(2):
                                for bb in range(4):
                                    c = (hb * 4 + bb) * 128
                                    mm = pe.matmul(out, (qpad0, qpad1)[a][:, hp, c:c + 128], kxs[hb][:, hp, bb, :],
                                                   start=(hb == 0 and hp == 0 and bb == 0),
                                                   stop=(hb == 1 and hp == 1 and bb == 3))
                mm.then_inc(g_s, 1)

            def turn_p(j):
                pe.wait_ge(g_p, j + 1)
                take(tfree)
                for u in range(units(j)):
                    for t in range(width(j) // 128):
                        mm = pe.transpose(tps[:, t, u * 128:(u + 1) * 128], sm[j % 3][:, u, t * 128:(t + 1) * 128], ident)
                    if GR[j][0] == "ss":
                        mm = pe.transpose(tps[0:NS, 1, u * 128:(u + 1) * 128], sm[j % 3][:, u, 160:192], ident)
                mm.then_inc(g_t, 1)
                tfree[0] = (g_pt, j + 1)

            def values(j):
                kind, a, b = GR[j]
                if kind in ("ss", "sx"):
                    return
                pe.wait_ge(g_pt, j + 1)
                if j < 2:
                    pe.wait_ge(v_out, 6)
                    take(ofree)
                if prod_need.get(GR[j]) is not None:
                    pe.wait_ge(*out_of_banks(prod_need[GR[j]]))
                probs = pt[:, j % 2]
                r = 64 * (b % 2)
                if kind == "swa":
                    tiles = [0] if a == 0 else [a - 1, a]
                    for i, t in enumerate(tiles):
                        mm = pe.matmul(ops[r:r + 64, b // 2, 0:384], vp[:, t, b * 64:(b + 1) * 64],
                                       probs[:, i, 0:384], start=(i == 0), stop=(i == len(tiles) - 1))
                else:
                    for i in range(2):
                        mm = pe.matmul(ops[r:r + 64, b // 2, 0:SEQ], memv[:, a, i, b * 64:(b + 1) * 64],
                                       probs[:, i, :], start=(i == 0), stop=(i == 1))
                if j in WITH_SX:
                    part = (j - WITH_SX[0]) % 2
                    mm = values_sx(0, range(4 * part, 4 * part + 4), [b // 2])
                if b % 2 == 1:
                    mm.then_inc(g_o, 1)

            def values_ss(hp):
                pe.wait_ge(g_pt, J_SS + 1)
                pe.wait_ge(ld["vb"], 16)
                pe.wait_ge(*out_of_banks(prod_need[("ss", 0, hp)]))
                c0 = hp * SB * WROW
                pe.matmul(ops[:, hp, 0:SB * WROW], vn[0:NS, hp * 128:(hp + 1) * 128],
                          pts[0:NS, 1, c0:c0 + SB * WROW], start=True, stop=False, skip_group_check=True)
                for bb in range(SB):
                    mm = pe.matmul(ops[:, hp, bb * WROW:(bb + 1) * WROW], vb[:, bb, hp * 128:(hp + 1) * 128],
                                   pts[:, 0, c0 + bb * WROW:c0 + (bb + 1) * WROW],
                                   start=False, stop=(bb == SB - 1), skip_group_check=True)
                mm.then_inc(g_o, 1)

            def values_sx(l, samples, hps):
                j = J_SX[l]
                probs = (ptx[:, :, :], pt[:, j % 2])[l]
                pe.wait_ge(g_pt, j + 1)
                if l == 1 and samples[0] == 0:
                    pe.wait_ge(*out_of_banks(prod_need[GR[j]]))
                for hb in sorted({s_ // 4 for s_ in samples}):
                    pe.wait_ge(ld[f"vx{hb}"], 16 * (l + 1))
                for s_ in samples:
                    for hp in hps:
                        for t in range(2):
                            mm = pe.matmul(ops[:, hp, XCOL + s_ * 16:XCOL + s_ * 16 + 16],
                                           vxs[s_ // 4][:, t, s_ % 4, hp * 128:(hp + 1) * 128],
                                           probs[:, t, s_ * 16:s_ * 16 + 16], start=(t == 0), stop=(t == 1))
                return mm

            def attention_0():
                for j in range(2, G_L1 + 3):
                    if j < G_L1:
                        scores(j)
                    if j == 2:
                        turn_v(1)
                    if j - 2 < G_L1:
                        turn_p(j - 2)
                    if 0 <= j - 3 < G_L1:
                        values(j - 3)
                    if j - 3 in (J_SS, J_SS + 4):
                        values_ss((j - 3 - J_SS) // 4)

            def out_proj(q0, l, ready, order):
                for m in range(8):
                    if m == 0:
                        panel(q0, 0, *act_hl[l], ready=ready, order=order)
                    else:
                        panel(q0 + m // 4, m % 4, *act_hl[l])

            def mlp_group(q, l, u0, first=None, stat=None):
                for m in range(8):
                    panel(q + m // 4, m % 4, *act_hl[1 - l], ready=first if m == 0 else None)
                    if m == 0 and stat:
                        colsum(stat, NT)
                for m in range(8):
                    panel(q + (2 + m // 4), m % 4, *act_hl[l], ready=(lambda k: (u_lo, u0 + (k + 1))) if m == 0 else None)

            def mlp(q0, l, first, stat):
                mlp_group(q0, l, 32 * l, first, stat)
                with pe.Fori(1, GROUPS) as g:
                    mlp_group(g * 4 + q0, l, g * 8 + 32 * l)

            def normed(n):
                return lambda k: (a_los, 8 * n + k + 1)

            pe.wait_ge(ld["con2"], 16)
            colsum(1, NMEM)
            for l in range(2):
                for p in range(4):
                    panel(Q_MEM + l, p, *act_hl[1], l * NMEM, (l + 1) * NMEM,
                          ready=(lambda k: (m_los[l], k + 1)) if p == 0 else None, guard=l > 0 or p >= 2)
                    if p in (1, 2):
                        headsum(2 * l + p - 1)
                    if p == 3:
                        turn_memv(2 * l)
                    if (l, p) == (1, 0):
                        turn_memv(1)
            for i in range(12):
                panel(Q_ATT + i // 4, i % 4, *act_hl[0], ready=normed(0) if i == 0 else None)
                if i == 0:
                    turn_memv(3)
                    colsum(2, NT)
                if 1 <= i <= 10:
                    headsum(N_ATT + i - 1)
                if i == 10:
                    scores(0)
                    scores(1)
                if i == 11:
                    turn_v(0)
            attention_0()
            out_proj(Q_OUT0, 0, lambda k: (g_olo, O0_READY[k]), range(KC))
            mlp(Q_MLP0, 0, normed(1), 3)

            def chunk_read(k, mm):
                if k < EARLY:
                    mm.then_inc(c_read, 1)

            def between_sx(k, _mm):
                mm = values_sx(1, (k,), (0, 1))
                if k == SB - 1:
                    mm.then_inc(g_o, 1)

            for i in range(20):
                panel(Q_CONV + i // 4, i % 4, *act_hl[1], ready=normed(2) if i == 0 else None,
                      between=between_sx if i == at_s(J_SX[1]) + 4 else chunk_read if i == 19 else None)
                if i == 0:
                    colsum(4, NT)
                if i in (1, 2):
                    headsum(N_QX[1] + i - 1)
                for j in L1:
                    if i == at_s(j) + 2:
                        turn_p(j)
                    if i == at_s(j) + 3 and j != J_SX[1]:
                        values(j)
                for j in L1:
                    if i == at_s(j):
                        scores(j)
            out_proj(Q_OUT1, 1, lambda j: (c_lo, j + 1), O1_ORDER)
            mlp(Q_MLP1, 1, normed(3), 5)

        @block.vector
        def _(dve):
            chained = [0]

            def link(ins):
                chained[0] += 1
                ins.then_inc(ch, 1)
                dve.wait_ge(ch, chained[0])

            def split_lo(q, d):
                dve.wait_ge(w_his[d], q + 1)
                dve.tensor_tensor(w_lo[:, d], stage[:, d], w_hi[:, d].bitcast(f32), ALU.subtract).then_inc(w_los[d], 1)

            def split_next(q, p):
                if p % 2 == 0 and next_duo(q, p):
                    split_lo(*next_duo(q, p))

            def take_scaled(q, p, out, cols=NT):
                full(dve, q, p)
                if cols > 512:
                    ins = dve.tensor_tensor(halves(out), zp(p % 2), halves(rstd[:, :]), ALU.mult)
                else:
                    ins = dve.tensor_tensor(out, zps[p % 2][:, 0, 0:cols], rstd[:, 0:cols], ALU.mult)
                ins.then_inc(z_free[p % 2], 1)

            def inv_rms(n, cols):
                dve.wait_ge(s_sd, n)
                dve.reciprocal(rstd[:, 0:cols], tmp[:, 2, 0:cols]).then_inc(s_rstd, 1)
                dve.wait_ge(s_rstd, n)

            def head_norm(n):
                kind, l, i = NORMS[n]
                cols = norm_cols(n)
                dve.wait_ge(n_sd, n + 1)
                taken(dve, *norm_panel(n))
                link(dve.reciprocal(tmp[:, 3, 0:cols], tmp[:, 2, 0:cols]))
                src = norm_src(n)
                if kind == "mem":
                    dve.wait_ge(zeroed, 1)
                    for hf in range(2):
                        r = slice(64 * hf, 64 * hf + 64)
                        ins = dve.scalar_tensor_tensor(out=memkz[r, l, 2 * i + hf, :], in0=src[r],
                                                       scalar=hgain(norm_gain(n), r.start, r.stop),
                                                       in1=tmp[r, 3, 0:cols], op0=ALU.mult, op1=ALU.mult)
                else:
                    ins = dve.scalar_tensor_tensor(out=src, in0=src, scalar=hgain(norm_gain(n)), in1=tmp[:, 3, :],
                                                   op0=ALU.mult, op1=ALU.mult)
                ins.then_inc(n_out, 1)

            def spread_keys(r):
                dve.wait_ge(r_out, r + 1)
                dve.wait_ge(zeroed, 2)
                for hf in range(2):
                    s = slice(64 * hf, 64 * hf + 64)
                    ins = dve.tensor_copy(kz[s, 2 * r + hf, :], z0[s, r, 0:SEQ])
                ins.then_inc(kz_rdy, 1)

            def turned_memv(n):
                l, c = n // 2, n % 2
                dve.wait_ge(v_t, n + 1)
                dve.tensor_copy(memv[:, l, :, c * 128:(c + 1) * 128], ops[:, :, 0:128]).then_inc(v_out, 1)

            def norm_lo(n, k, norm):
                dve.wait_ge(a_his, 8 * n + k + 1)
                hi, lo = act_hl[NORM_TO[n]]
                dve.scalar_tensor_tensor(out=lo[:, k, :], in0=X[:, k, :], scalar=gain(norm, k),
                                         in1=hi[:, k, :].bitcast(f32), op0=ALU.mult, op1=ALU.subtract).then_inc(a_los, 1)

            def residual(q, m):
                p = m % 4
                full(dve, q + m // 4, p)
                dve.wait_ge(z_free[p % 2], (q + m // 4) * 2 + p // 2)
                dve.tensor_tensor(halves(X[:, m, :]), zp(p % 2), halves(X[:, m, :]), ALU.add).then_inc(z_free[p % 2], 1)

            def maxes(j):
                kind, a, b = GR[j]
                n, w = units(j), width(j)
                dve.wait_ge(g_s, j + 1)
                if j >= 3:
                    dve.wait_ge(g_t, j - 2)
                n0 = first_sink(j)
                for u in range(n):
                    if kind == "swa":
                        mask = con[:, C_MASKP + 256 - w:C_MASKP + 256]
                    elif kind == "ss":
                        mask = con[:, C_MASKS:C_MASKS + 132]
                    else:
                        mask = con[:, C_ZERO:C_ZERO + 1].broadcast_to([128, w])
                    first = 3.0e38 if n0 is None else nsink[:, n0 + u:n0 + u + 1]
                    ins = dve.tensor_tensor_reduce(out=sm[j % 3][:, u, 0:w], in0=score_cols(j, u), in1=mask, scale=-SCALE, scalar=first,
                                                   op0=ALU.add, op1=ALU.min, accum_out=st[:, j % 3, 0, u:u + 1])
                ins.then_inc(g_max, 1)
                if n0 is not None:
                    dve.wait_ge(g_max, j + 1)
                    dve.tensor_tensor(st[:, j % 3, 2, 0:n], st[:, j % 3, 0, 0:n], nsink[:, n0:n0 + n],
                                      ALU.subtract).then_inc(g_sink, 1)

            def normalise(j):
                kind = GR[j][0]
                n, w, b = units(j), width(j), j % 3
                dve.wait_ge(g_exp, j + 1)
                total = st[:, b, 1, 0:n]
                if first_sink(j) is not None:
                    link(dve.tensor_tensor(st[:, b, 3, 0:n], total, st[:, b, 2, 0:n], ALU.add))
                    total = st[:, b, 3, 0:n]
                link(dve.reciprocal(st[:, b, 4, 0:n], total))
                for u in range(n):
                    ins = dve.tensor_scalar(sm[b][:, u, 0:w], sm[b][:, u, 0:w], st[:, b, 4, u:u + 1], None, ALU.mult)
                if kind == "ss":
                    link(ins)
                    for u in range(n):
                        own = sm[b][:, u, 128:132].unsqueeze(1).broadcast_to([128, SB, ST])
                        blk = con[:, C_BLK + u % 2 * SB:C_BLK + (u % 2 + 1) * SB].unsqueeze(2).broadcast_to([128, SB, ST])
                        ins = dve.tensor_tensor(sm[b][:, u, 160:192].rearrange("p (b t) -> p b t", b=SB), own, blk, ALU.mult)
                ins.then_inc(g_p, 1)

            def product_lo(n):
                dve.wait_ge(g_ohi, n + 1)
                hi, lo = act_hl[0]
                for dst, src in product_parts(n):
                    ins = dve.tensor_tensor(dst(lo, 0), src, dst(hi, 0).bitcast(f32), ALU.subtract)
                ins.then_inc(g_olo, 1)

            def attention_0():
                for j in range(2, G_L1 + 4):
                    if j == J_SX[0]:
                        split_lo(Q_OUT0, 0)
                    if j < G_L1:
                        maxes(j)
                    if 0 <= j - 4 < G_L1:
                        for n in products_at(j - 4):
                            product_lo(n)
                    if j - 1 < G_L1:
                        normalise(j - 1)

            def out_proj(q0, n, norm):
                for m in range(8):
                    split_next(q0 + m // 4, m % 4)
                    residual(q0, m)
                    taken(dve, q0 + m // 4, m % 4)
                    norm_lo(n, m, norm)

            def hidden_lo(l, u, m):
                dve.wait_ge(u_hi, u + 1)
                hi, lo = act_hl[l]
                dve.tensor_tensor(lo[:, m, :], tmp[:, 3 + m % 2, :], hi[:, m, :].bitcast(f32),
                                  ALU.subtract).then_inc(u_lo, 1)

            def mlp_group(q, l, u0, first=False, stat=None, then=None):
                for m in range(8):
                    split_next(q + m // 4, m % 4)
                    full(dve, q + m // 4, m % 4)
                    if m == 0 and stat:
                        inv_rms(stat, NT)
                    if m >= 2 or not first:
                        dve.wait_ge(u_sq, u0 + (m - 1))
                    dve.scalar_tensor_tensor(out=halves(tmp[:, m % 2, :]), in0=zp(m % 2), scalar=0.0,
                                             in1=halves(rstd[:, :]), op0=ALU.max, op1=ALU.mult).then_inc(z_free[m % 2], 1)
                    if m >= 1:
                        hidden_lo(l, u0 + (m - 1), m - 1)
                hidden_lo(l, u0 + 7, 7)
                for m in range(8):
                    split_next(q + (2 + m // 4), m % 4)
                    residual(q + 2, m)
                    if then:
                        taken(dve, q + 2 + m // 4, m % 4)
                        norm_lo(then[0], m, then[1])

            def mlp(q0, l, stat, then):
                mlp_group(q0, l, 32 * l, first=l == 0, stat=stat)
                with dve.Fori(1, GROUPS - 1) as g:
                    mlp_group(g * 4 + q0, l, g * 8 + 32 * l)
                mlp_group(q0 + 4 * (GROUPS - 1), l, 32 * l + 8 * (GROUPS - 1), then=then)

            def memory_lo(k):
                l, cols = 0, slice(0, NMEM)
                dve.wait_ge(m_hi, k + 1)
                dve.scalar_tensor_tensor(out=act_hl[1][1][:, k, cols], in0=memx[:, k, :], scalar=gain(4 + l, k),
                                         in1=act_hl[1][0][:, k, cols].bitcast(f32), op0=ALU.mult,
                                         op1=ALU.subtract).then_inc(m_los[l], 1)

            dve.wait_ge(ld["con"], 16)
            dve.wait_ge(ld["mem0"], 16)
            for k in range(KC):
                memory_lo(k)
            for half, made, done in ((0, w_his_half, w_los_half), (1, w_his[0], w_los[0])):
                dve.wait_ge(made, 1)
                c = slice(half * 128, half * 128 + 128)
                dve.tensor_tensor(w_lo[:, 0, :, c], stage[:, 0, :, c], w_hi[:, 0, :, c].bitcast(f32), ALU.subtract).then_inc(done, 1)
            link(dve.tensor_scalar(nsink[:, :], con[:, C_SINK:C_SINK + 16], -1.0, None, ALU.mult))
            split_lo(0, 1)
            inv_rms(1, NMEM)
            for l in range(2):
                for p in range(4):
                    q = Q_MEM + l
                    if (l, p) != (0, 0):
                        split_next(q, p)
                    take_scaled(q, p, tmp[:, 4 + p // 2, (p % 2) * 256:(p % 2) * 256 + 256], NMEM)
                    norm_lo(0, 4 * l + p, 0)
                    if p in (1, 2):
                        head_norm(2 * l + p - 1)
                    if p == 3:
                        turned_memv(2 * l)
                    if (l, p) == (1, 0):
                        turned_memv(1)
            dve.wait_ge(ld["rope"], 16)
            dve.wait_ge(ld["con2"], 16)
            for i in range(12):
                q, p = Q_ATT + i // 4, i % 4
                if i == 0:
                    turned_memv(3)
                    inv_rms(2, NT)
                take_scaled(q, p, z0[:, i, :])
                if i < 10:
                    split_next(q, p)
                if i == 10:
                    maxes(0)
                    maxes(1)
                if 1 <= i <= 10:
                    head_norm(N_ATT + i - 1)
                if i in (5, 6):
                    spread_keys(i - 5)
                if i == 11:
                    normalise(0)
            attention_0()
            dve.wait_ge(b_out, 16)
            out_proj(Q_OUT0, 1, 2)
            mlp(Q_MLP0, 0, 3, (2, 1))
            def mixer_lo(n):
                c = O1_ORDER[n]
                dve.wait_ge(c_hi, n + 1)
                src = oconv[:, c, :] if c < 6 else ocross[:, c - 6, :]
                dve.tensor_tensor(act_hl[1][1][:, c, :], src, act_hl[1][0][:, c, :].bitcast(f32), ALU.subtract).then_inc(c_lo, 1)

            for i in range(20):
                q, p = Q_CONV + i // 4, i % 4
                split_next(q, p)
                if i == 19:
                    for n in range(EARLY):
                        mixer_lo(n)
                if i == 0:
                    inv_rms(4, NT)
                if i < 2:
                    take_scaled(q, p, z1[:, i, :])
                else:
                    c, what = (i - 2) // 3, (i - 2) % 3
                    if what == 0 and c:
                        dve.wait_ge(c_o, c)
                    take_scaled(q, p, tmp[:, 4 if what != 1 else 5, :])
                    taken(dve, q, p)
                    if what == 1:
                        if c < 2:
                            link(dve.memset(vconv[:, c, 0:2], 0.0))
                        if c == 0:
                            link(dve.tensor_copy(sconv[:, :, :, 0:2], con[:, C_ST:C_ST + 96].rearrange(
                                "p (c b t) -> p c b t", c=CONVC, b=SB)))
                        v = vconv[:, c % 2]
                        by_b = (lambda ap: ap.rearrange("p (b t) -> p b t", b=SB))
                        dve.tensor_tensor(v[:, 2:SEQ + 2], tmp[:, 4, 0:SEQ], tmp[:, 5, 0:SEQ], ALU.mult)
                        link(dve.tensor_tensor(sconv[:, c, :, 2:ST + 2], by_b(tmp[:, 4, SEQ:NT]), by_b(tmp[:, 5, SEQ:NT]), ALU.mult))
                        y, ys = tmp[:, 0, 0:SEQ], by_b(tmp[:, 0, SEQ:NT])
                        dve.tensor_copy(tails[:, c, :], v[:, SEQ:SEQ + 2]).then_inc(c_tail, 1)
                        dve.tensor_scalar(y, v[:, 0:SEQ], tap(0, c), None, ALU.mult)
                        link(dve.tensor_scalar(ys, sconv[:, c, :, 0:ST], tap(0, c), None, ALU.mult))
                        for j in (1, 2):
                            dve.scalar_tensor_tensor(out=y, in0=v[:, j:SEQ + j], scalar=tap(j, c), in1=y,
                                                     op0=ALU.mult, op1=ALU.add)
                            link(dve.scalar_tensor_tensor(out=ys, in0=sconv[:, c, :, j:ST + j], scalar=tap(j, c), in1=ys,
                                                          op0=ALU.mult, op1=ALU.add))
                    if what == 2:
                        dve.tensor_tensor(oconv[:, c, :], tmp[:, 4, :], tmp[:, 0, :], ALU.mult).then_inc(c_o, 1)
                if i in (1, 2):
                    head_norm(N_QX[1] + i - 1)
                for j in L1:
                    if i == at_s(j):
                        maxes(j)
                    if i == at_s(j) + 1:
                        normalise(j)
            dve.wait_ge(c_o, CONVC)
            for n in range(EARLY, KC):
                mixer_lo(n)
            dve.wait_ge(b_out, 48)
            out_proj(Q_OUT1, 3, 3)
            mlp(Q_MLP1, 1, 5, None)

        @block.scalar
        def _(act):
            sd_free = [None]

            def copy(out, in_, **kw):
                return act.activation(out, in_, ACT.Copy, **kw)

            def split_hi(q, d, first=False):
                act.wait_ge(w_in[d], q * 16 + 16)
                if not first:
                    act.wait_ge(z_full[1], q * 2 + (d - 1))
                copy(w_hi[:, d], stage[:, d]).then_inc(w_his[d], 1)

            def split_next(q, p):
                if p % 2 == 0 and next_duo(q, p):
                    split_hi(*next_duo(q, p), first=isinstance(q, int) and next_duo(q, p)[0] == 0)

            def root(src, dst, mean_of, sem_in, n, sem_out, free):
                act.wait_ge(sem_in, n)
                if sd_free[0]:
                    act.wait_ge(*sd_free[0])
                act.activation(dst, src, ACT.Sqrt, bias=eps, scale=1.0 / mean_of).then_inc(sem_out, 1)
                sd_free[0] = free

            def root_tokens(n, cols):
                src, dst = (tps[:, :, 0:HALF], halves(tmp[:, 2, :])) if cols > 512 else (tps[:, 0, 0:cols], tmp[:, 2, 0:cols])
                root(src, dst, D, s_full, n, s_sd, (s_rstd, n))

            def root_heads(n):
                cols = norm_cols(n)
                src, dst = (tps[:, :, 0:HALF], halves(tmp[:, 2, :])) if cols > 512 else (tps[:, 0, 0:cols], tmp[:, 2, 0:cols])
                root(src, dst, HD, n_ms, n + 1, n_sd, (n_out, n + 1))

            def square(n):
                taken(act, *norm_panel(n))
                if n >= 2:
                    act.wait_ge(n_ms, n - 1)
                act.activation(tmp[:, n % 2, 0:norm_cols(n)], norm_src(n), ACT.Square).then_inc(n_sq, 1)

            def norm_hi(n, k, norm):
                copy(act_hl[NORM_TO[n]][0][:, k, :], X[:, k, :], scale=gain(norm, k)).then_inc(a_his, 1)

            def exps(j):
                b, n, w = j % 3, units(j), width(j)
                act.wait_ge(g_max, j + 1)
                for u in range(n):
                    ins = act.activation(sm[b][:, u, 0:w], sm[b][:, u, 0:w], ACT.Exp, bias=st[:, b, 0, u:u + 1],
                                         scale=-1.0, accum_out=st[:, b, 1, u:u + 1])
                if first_sink(j) is not None:
                    act.wait_ge(g_sink, sum(first_sink(i) is not None for i in range(j + 1)))
                    ins = act.activation(st[:, b, 2, 0:n], st[:, b, 2, 0:n], ACT.Exp)
                ins.then_inc(g_exp, 1)

            def probs_out(j):
                kind, a, g = GR[j]
                b = j % 2
                act.wait_ge(g_t, j + 1)
                n = units(j) * 128
                if kind == "ss":
                    own = (lambda ap, r: ap.rearrange("p (u r) -> p u r", r=r)[:, :, 0:4 * WROW])
                    copy(own(pts[:, 0, :], 4 * WROW), own(tps[:, 0, :], 128))
                    ins = copy(own(pts[0:NS, 1, :], 4 * WROW), own(tps[0:NS, 1, :], 128))
                elif j == J_SX[0]:
                    ins = copy(ptx[:, :, :], tps[:, :, 0:128])
                elif width(j) == 128:
                    ins = copy(pt[:, b, 0, 0:n], tps[:, 0, 0:n])
                else:
                    ins = copy(pt[:, b, :, 0:n], tps[:, :, 0:n])
                ins.then_inc(g_pt, 1)

            def product_out(n):
                act.wait_ge(g_o, n + 1)
                if n == P_L0:
                    act.wait_ge(vn_out, 32)
                for dst, src in product_parts(n):
                    ins = copy(dst(act_hl[0][0], 0) if n < P_L0 else dst(ocross, 6), src)
                ins.then_inc(g_ohi, 1)

            def turned_v(c):
                act.wait_ge(v_t, 5 + c)
                copy(vp[:, :, c * 128:(c + 1) * 128], ops[:, 0, :].rearrange("p (t d) -> p t d", t=4))
                copy(vn[0:NS, c * 128:(c + 1) * 128], ops[0:NS, 1, 0:128]).then_inc(v_out, 1)

            def attention_0():
                for j in range(2, G_L1 + 3):
                    if j == 2:
                        turned_v(1)
                    if j - 2 < G_L1:
                        probs_out(j - 2)
                    if j < G_L1:
                        exps(j)
                    if 0 <= j - 3 < G_L1:
                        for n in products_at(j - 3):
                            product_out(n)

            def out_proj(q0, n, norm):
                for m in range(8):
                    split_next(q0 + m // 4, m % 4)
                    taken(act, q0 + m // 4, m % 4)
                    norm_hi(n, m, norm)

            def mlp_group(q, l, u0, first=False, stat=None, then=None, last=False):
                for m in range(8):
                    split_next(q + m // 4, m % 4)
                    if m == 0 and stat:
                        root_tokens(stat, NT)
                    taken(act, q + m // 4, m % 4)
                    if m >= 2 or not first:
                        act.wait_ge(u_lo, u0 + (m - 1))
                    act.activation(tmp[:, 3 + m % 2, :], tmp[:, m % 2, :], ACT.Square).then_inc(u_sq, 1)
                    act.wait_ge(u_sq, u0 + (m + 1))
                    copy(act_hl[l][0][:, m, :], tmp[:, 3 + m % 2, :]).then_inc(u_hi, 1)
                for m in range(8):
                    split_next(q + (2 + m // 4), m % 4)
                    if then is not None:
                        taken(act, q + 2 + m // 4, m % 4)
                        norm_hi(then[0], m, then[1])
                    if last:
                        taken(act, q + 2 + m // 4, m % 4)
                        act.dma_start(yT[:, m, :], X[:, m, :]).then_inc(y_out, 16)

            def mlp(q0, l, stat, then, last):
                mlp_group(q0, l, 32 * l, first=l == 0, stat=stat)
                with act.Fori(1, GROUPS - 1) as g:
                    mlp_group(g * 4 + q0, l, g * 8 + 32 * l)
                mlp_group(q0 + 4 * (GROUPS - 1), l, 32 * l + 8 * (GROUPS - 1), then=then, last=last)

            def memory_hi(l, k):
                copy(act_hl[1][0][:, k, l * NMEM:(l + 1) * NMEM], memx[:, k, :], scale=gain(4 + l, k)).then_inc(m_hi, 1)

            act.dma_start(con[:, 0:C_IDENT], cst[:, 0:C_IDENT]).then_inc(ld["con"], 16)
            def swapped(r):
                act.wait_ge(n_out, N_ATT + r + 1)
                if r >= 2:
                    act.wait_ge(r_out, r - 1)
                for to in range(0, 128, 32):
                    act.dma_start(tmp[to:to + 32, 4 + r % 2, :], z0[to ^ 32:(to ^ 32) + 32, r, :]).then_inc(r_sw[r % 2], 16)

            def memory_full(k):
                act.wait_ge(sq_acc, 1)
                copy(msq[:, k, :], memx[:, k, :], scale=gain(5, k)).then_inc(m_full, 1)

            act.wait_ge(ld["con"], 16)
            act.wait_ge(ld["mem0"], 16)
            for k in range(4):
                memory_hi(0, k)
            act.wait_ge(ld["mem1"], 16)
            act.dma_start(con[:, C_IDENT:C_N], cst[:, C_IDENT:C_N]).then_inc(ld["con2"], 16)
            act.dma_start(X[:, :, :], xT).then_inc(ld["x"], 16)
            act.dma_start(cs[:, :, :], rope).then_inc(ld["rope"], 16)
            for k in range(4, KC):
                memory_hi(0, k)
            act.wait_ge(w_in[0], 16)
            copy(w_hi[:, 0, :, 0:128], stage[:, 0, :, 0:128]).then_inc(w_his_half, 1)
            copy(w_hi[:, 0, :, 128:DUO], stage[:, 0, :, 128:DUO]).then_inc(w_his[0], 1)
            memory_hi(1, 0)
            memory_hi(1, 1)
            split_hi(0, 1, first=True)
            act.wait_ge(ld["con2"], 16)
            memory_full(0)
            root_tokens(1, NMEM)
            memory_full(1)
            for k in range(2, KC):
                memory_hi(1, k)
                memory_full(k)
            act.wait_ge(ld["x"], 16)
            for l in range(2):
                for p in range(4):
                    if (l, p) != (0, 0):
                        split_next(Q_MEM + l, p)
                    norm_hi(0, 4 * l + p, 0)
                    if p < 2:
                        square(2 * l + p)
                    if p in (1, 2):
                        root_heads(2 * l + p - 1)
            for i in range(12):
                split_next(Q_ATT + i // 4, i % 4)
                if i == 0:
                    root_tokens(2, NT)
                if i < 10:
                    square(N_ATT + i)
                if 1 <= i <= 10:
                    root_heads(N_ATT + i - 1)
                if 2 <= i <= 9:
                    swapped(i - 2)
                if i == 10:
                    exps(0)
                    exps(1)
                if i == 11:
                    turned_v(0)
            attention_0()
            act.wait_ge(b_out, 16)
            out_proj(Q_OUT0, 1, 2)
            mlp(Q_MLP0, 0, 3, (2, 1), False)
            def mixer_hi(n):
                c = O1_ORDER[n]
                if c < 6:
                    act.wait_ge(c_o, c + 1)
                if n < EARLY:
                    act.wait_ge(c_read, n + 1)
                copy(act_hl[1][0][:, c, :], oconv[:, c, :] if c < 6 else ocross[:, c - 6, :]).then_inc(c_hi, 1)

            for i in range(20):
                split_next(Q_CONV + i // 4, i % 4)
                if i == 19:
                    for n in range(EARLY):
                        mixer_hi(n)
                if i == 0:
                    root_tokens(4, NT)
                if i < 2:
                    square(N_QX[1] + i)
                if i in (1, 2):
                    root_heads(N_QX[1] + i - 1)
                for j in L1:
                    if i == at_s(j):
                        exps(j)
                    if i == at_s(j) + 2:
                        probs_out(j)
                    if i == at_s(j) + (4 if j == J_SX[1] else 3):
                        for n in products_at(j):
                            product_out(n)
            full(act, Q_OUT1 - 1, 3)
            act.wait_ge(g_ohi, len(PRODUCT))
            for n in range(EARLY, KC):
                mixer_hi(n)
            act.wait_ge(b_out, 48)
            out_proj(Q_OUT1, 3, 3)
            mlp(Q_MLP1, 1, 5, None, True)
            act.wait_ge(y_out, 16 * 8)

        @block.gpsimd
        def _(pool):
            n_chain = [0]

            def link(ins):
                n_chain[0] += 1
                ins.then_inc(pool_ch, 1)
                pool.wait_ge(pool_ch, n_chain[0])

            def sum_squares(n, src, cols, before):
                if n > 1:
                    pool.wait_ge(s_full, n - 1)
                for k in range(KC):
                    before(k)
                    x = src[:, k, 0:cols]
                    if k == 0:
                        link(pool.tensor_tensor(pacc[:, 0:cols], x, x, ALU.mult))
                        continue
                    link(pool.tensor_tensor(psq[:, 0:cols], x, x, ALU.mult))
                    ins = pool.tensor_tensor(pacc[:, 0:cols], pacc[:, 0:cols], psq[:, 0:cols], ALU.add)
                    if k < KC - 1:
                        link(ins)
                ins.then_inc(sq_acc, 1)
                pool.wait_ge(sq_acc, n)

            def spread_queries(src, dst):
                for h in range(4):
                    r = slice(64 * (h % 2), 64 * (h % 2) + 64)
                    ins = pool.tensor_copy(dst[r, h // 2, :].rearrange("p (b r) -> p b r", r=144)[:, :, h * 4:h * 4 + 4],
                                           src(h // 2)[r, SEQ:NT].rearrange("p (b t) -> p b t", b=SB))
                ins.then_inc(qp_rdy, 1)

            pool.memset(memkz[:, :, :, :], 0.0).then_inc(zeroed, 1)
            for i in range(2):
                pool.wait_ge(ld[f"mem{i}"], 16)
                m = memx[:, 4 * i:4 * i + 4, :]
                link(pool.tensor_tensor(msq[:, 4 * i:4 * i + 4, :], m, m, ALU.mult))
            for n in (4, 2):
                link(pool.tensor_tensor(msq[:, 0:n, :], msq[:, 0:n, :], msq[:, n:2 * n, :], ALU.add))
            pool.tensor_tensor(pacc[:, 0:NMEM], msq[:, 0, :], msq[:, 1, :], ALU.add).then_inc(sq_acc, 1)
            for k in range(KC):
                pool.wait_ge(m_full, k + 1)
                pool.tensor_tensor(act_hl[1][1][:, k, NMEM:2 * NMEM], msq[:, k, :],
                                   act_hl[1][0][:, k, NMEM:2 * NMEM].bitcast(f32), ALU.subtract).then_inc(m_los[1], 1)
            pool.wait_ge(ld["x"], 16)
            sum_squares(2, X, NT, lambda k: None)
            pool.dma_start(vb[:, :, :], swav).then_inc(ld["vb"], 16)
            for l in range(2):
                pool.wait_ge(m_los[l], KC)
            pool.wait_ge(m_hi, 16)
            pool.dma_start(kt[:, :, :, 0:128], swakT).then_inc(ld["kt"], 16)
            for p in (2, 3):
                full(pool, Q_ATT - 1, p)
            pool.memset(kz[:, :, :], 0.0).then_inc(zeroed, 1)
            pool.wait_ge(ld["rope"], 16)
            for r in range(8):
                pool.wait_ge(r_sw[r % 2], 64 * (r // 2 + 1))
                z, other = z0[:, r, :], tmp[:, 4 + r % 2, :]
                pool.tensor_tensor(z, z, cs[:, 0, :], ALU.mult)
                link(pool.tensor_tensor(other, other, cs[:, 1, :], ALU.mult))
                pool.tensor_tensor(z, z, other, ALU.add).then_inc(r_out, 1)
            pool.wait_ge(r_out, 8)
            pool.wait_ge(ld["kt"], 16)
            for hp in range(2):
                pool.tensor_copy(kt[:, hp, :, 128:132], z0[:, hp, SEQ:NT].rearrange("p (b t) -> p b t", b=SB)).then_inc(kt_new, 1)
            pool.wait_ge(n_out, N_QX[0] + 2)
            link(pool.memset(qwin[:, :, :], 0.0))
            for c in range(6):
                for hf in range(2):
                    r, at = slice(64 * hf, 64 * hf + 64), (hf * GRP + c % GRP) * ST
                    ins = pool.tensor_copy(qwin[r, c // GRP * SB:(c // GRP + 1) * SB, at:at + ST],
                                           z0[r, 2 + c, SEQ:NT].rearrange("p (b t) -> p b t", b=SB))
            ins.then_inc(qp_rdy, 1)
            pool.wait_ge(kt_new, 2)
            pool.dma_start(o_ks, kt[:, :, :, ST:132]).then_inc(win_out, 16)
            pool.dma_start(o_kp, z0[:, 0:2, SEQ - 128:SEQ]).then_inc(b_out, 16)
            pool.wait_ge(ld["vb"], 16)
            pool.dma_start(o_vs.rearrange("b s d -> s b d"), vb[ST:128, :, :]).then_inc(win_out, 16)
            pool.wait_ge(v_out, 6)
            pool.dma_start(o_vn, vn[0:NS, :]).then_inc(vn_out, 16)
            pool.dma_start(o_vp, vp[:, 3, :]).then_inc(vn_out, 16)
            pool.wait_ge(g_s, J_SS + 1)
            pool.wait_ge(win_out, 32)
            pool.dma_start(kxs[0][:, :, :, :], xkT[0, 0]).then_inc(ld["kx0"], 16)
            link(pool.memset(qpad0[:, :, :], 0.0))
            spread_queries(lambda hp: z0[:, 8 + hp, :], qpad0)
            pool.wait_ge(g_o, PRODUCT.index(("ss", 0, 1)) + 1)
            pool.dma_start(kxs[1][:, :, :, :], xkT[0, 1]).then_inc(ld["kx1"], 16)
            for l in range(2):
                if l == 1:
                    pool.wait_ge(n_out, N_QX[1] + 2)
                    link(pool.memset(qpad1[:, :, :], 0.0))
                    spread_queries(lambda hp: z1[:, hp, :], qpad1)
                pool.wait_ge(g_s, J_SX[l] + 1)
                for i in range(2):
                    pool.dma_start(vxs[i][:, :, :, :], xv[l, i]).then_inc(ld[f"vx{i}"], 16)
                if l == 0:
                    for i in range(2):
                        for h in range(NXH):
                            r = slice(64 * (h % 2), 64 * (h % 2) + 64)
                            pool.dma_start(o_mk[i, h], memkz[r, i, h, :]).then_inc(stored, 16)
                        pool.dma_start(o_mv[i], memv[:, i, :, :]).then_inc(stored, 16)
                    pool.wait_ge(g_o, PRODUCT.index(GR[WITH_SX[-1]]) + 1)
                    for i in range(2):
                        pool.dma_start(kxs[i][:, :, :, :], xkT[1, i]).then_inc(ld[f"kx{i}"], 16)
                    sum_squares(3, X, NT, lambda k: taken(pool, Q_OUT0 + k // 4, k % 4))
                    sum_squares(4, X, NT, lambda k: taken(pool, Q_CONV - 2 + k // 4, k % 4))
            pool.wait_ge(c_tail, CONVC)
            pool.dma_start(o_cp, tails[:, :, :]).then_inc(b_out, 16)
            pool.dma_start(o_cs, sconv[:, :, :, ST:ST + 2]).then_inc(b_out, 16)
            sum_squares(5, X, NT, lambda k: taken(pool, Q_OUT1 + k // 4, k % 4))
            pool.wait_ge(vn_out, 32)
            pool.wait_ge(b_out, 48)
            pool.wait_ge(stored, 16 * 10)


def kernel(**inputs):
    from concourse import bacc
    from concourse.bass_utils import run_bass_kernel_spmd

    x = {k: np.asarray(v) for k, v in inputs.items()}

    def duos(w):
        return w.reshape(KC, 128, -1, DUO).transpose(2, 1, 0, 3)

    def feat(a):
        return a.reshape(-1, KC, 128).transpose(2, 1, 0)

    order = [(2 * hp + hf) * GRP + g for hp in range(2) for g in range(GRP) for hf in range(2)]
    qcols = np.concatenate([np.arange(h * HD, (h + 1) * HD) for h in order])
    c0, c1, c2 = NQH * HD, (NQH + NKV) * HD, (NQH + 2 * NKV) * HD
    wa = x["w_in_att"][0]
    parts = [x["w_mem_kv"][0], x["w_mem_kv"][1],
             np.concatenate([wa[:, c0:c1], wa[:, qcols], wa[:, c2:], wa[:, c1:c2]], axis=1),
             np.concatenate([x["w_out"][0][qcols], x["w_out"][0][c0:]], axis=0)]

    def mlp(l):
        for g in range(GROUPS):
            parts.append(x["w_up"][l][:, g * D:(g + 1) * D])
            parts.append(x["w_down"][l][g * D:(g + 1) * D])

    mlp(0)
    wc = x["w_in_conv"][0]
    cc = CONVC * 128
    cols = [wc[:, 3 * cc:]]
    for c in range(CONVC):
        cols += [wc[:, s * cc + c * 128:s * cc + (c + 1) * 128] for s in (1, 2, 0)]
    parts += [np.concatenate(cols, axis=1), x["w_out"][1]]
    mlp(1)
    wst = np.concatenate([duos(p) for p in parts], axis=0)
    assert wst.shape[0] == 2 * QUADS

    con = np.zeros((128, C_N), np.float32)
    norms = [x["norm_mix"][0], x["norm_mix"][1], x["norm_mlp"][0], x["norm_mlp"][1], x["norm_mem"][0], x["norm_mem"][1]]
    for i, g in enumerate(norms):
        con[:, C_G + 8 * i:C_G + 8 * i + 8] = g.reshape(KC, 128).T
    heads = [x["q_norm_att"][0], x["k_norm_att"][0], x["q_norm_x"][0], x["q_norm_x"][1], x["k_norm_x"][0], x["k_norm_x"][1]]
    for i, g in enumerate(heads):
        con[:, C_HG + i] = np.tile(g, 2)
    con[:, C_CW:C_CW + 18] = x["conv_w"][0].reshape(3, CONVC, 128).transpose(2, 0, 1).reshape(128, 18)
    con[:, C_SINK:C_SINK + 12] = x["sinks"][0][None, :]
    row = np.arange(128) % WROW // ST
    for u in range(4):
        con[:, C_SROW + u] = x["sinks"][0].reshape(NKV, GRP)[u // 2 * 2 + row // GRP, row % GRP]
    p = np.arange(128)
    con[:, C_IDENT:C_IDENT + 128] = np.eye(128)
    con[:, C_ONES:C_ONES + 128] = 1.0
    con[:, C_HEAD:C_HEAD + 128] = p[:, None] // HD == p[None, :] // HD
    key = np.arange(256)[None, :]
    con[:, C_MASKP:C_MASKP + 256] = np.where((key > p[:, None]) & (key <= p[:, None] + 128), 0.0, NEG / SCALE)
    t, key = (p % ST)[:, None], np.arange(132)[None, :]
    con[:, C_MASKS:C_MASKS + 132] = np.where((key > t) & (key <= t + 128), 0.0, NEG / SCALE)
    for half in range(2):
        con[:, C_BLK + half * SB:C_BLK + (half + 1) * SB] = p[:, None] // WROW + 4 * half == np.arange(SB)[None, :]
    con[:, C_ST:C_ST + 96] = x["state_conv"][0].reshape(SB, 2, CONVC, 128).transpose(3, 2, 0, 1).reshape(128, 96)
    con[:, C_EPS] = EPS

    half = HD // 2
    inv = (np.float32(10000.0) ** (-np.arange(half, dtype=np.float32) * np.float32(2.0) / np.float32(HD))).astype(np.float32)
    pos = np.concatenate([np.arange(SEQ), np.tile(PAST + np.arange(ST), SB)]).astype(np.float32)
    ang = (pos[:, None] * inv[None, :]).astype(np.float32)
    cos, sin = np.cos(ang).T, np.sin(ang).T
    rope = np.stack([np.tile(cos, (4, 1)), np.concatenate([-sin, sin, -sin, sin])], axis=1).astype(np.float32)

    kc = x["cache_swa_k"][0].transpose(2, 3, 0, 1).reshape(2, 128, SB, 128).transpose(1, 0, 2, 3)
    vc = x["cache_swa_v"][0].reshape(SB, 128, NKV * HD).transpose(1, 0, 2)
    xk = x["cache_mem_k"].reshape(2, 2, 4, NMEM, 2, 128).transpose(0, 1, 5, 4, 2, 3)
    xv = x["cache_mem_v"].reshape(2, 2, 4, 2, 128, NXH * HD).transpose(0, 1, 4, 3, 2, 5)
    feeds = {
        "xT": feat(np.concatenate([x["x_prompt"][0], x["x_sample"].reshape(NS, D)])),
        "memT": feat(x["mem_prompt"][0]), "wst": wst, "cst": con, "rope": rope,
        "swakT": kc, "swav": vc, "xkT": xk, "xv": xv,
    }
    outs = {
        "yT": (128, KC, NT), "o_kp": (128, 2, 128), "o_vp": (128, 256), "o_cp": (128, CONVC, 2),
        "o_mk": (2, NXH, 64, NMEM), "o_mv": (2, 128, 2, 256), "o_ks": (128, 2, SB, 128),
        "o_vs": (SB, 124, 256), "o_vn": (NS, 256), "o_cs": (128, CONVC, SB, 2),
    }
    nc = bacc.Bacc("TRN2", target_bir_lowering=False, num_devices=1)
    f32 = mybir.dt.float32
    aps, arrays = {}, {}
    for name, a in feeds.items():
        arrays[name] = np.ascontiguousarray(a, dtype=a.dtype)
        aps[name] = nc.dram_tensor(name, arrays[name].shape, f32, kind="ExternalInput").ap()
    for name, shape in outs.items():
        aps[name] = nc.dram_tensor(name, shape, f32, kind="ExternalOutput").ap()
    build_kernel(nc, **aps)
    r = run_bass_kernel_spmd(nc, [arrays], core_ids=[0]).results[0]

    y = r["yT"].transpose(2, 1, 0).reshape(NT, D)
    kp = r["o_kp"].transpose(2, 1, 0).reshape(1, 1, 128, NKV, HD)
    vp = r["o_vp"].reshape(1, 1, 128, NKV, HD)
    cp = r["o_cp"].transpose(2, 1, 0).reshape(1, 1, 2, cc)
    mk = r["o_mk"].transpose(0, 3, 1, 2).reshape(2, 1, NMEM, NXH, HD)
    mv = r["o_mv"].transpose(0, 2, 1, 3).reshape(2, 1, NMEM, NXH, HD)
    ks = r["o_ks"].transpose(2, 3, 1, 0).reshape(1, SB, 128, NKV, HD)
    vs = np.concatenate([r["o_vs"], r["o_vn"].reshape(SB, ST, 256)], axis=1).reshape(1, SB, 128, NKV, HD)
    cs = r["o_cs"].transpose(2, 3, 1, 0).reshape(1, SB, 2, cc)
    return tuple(np.ascontiguousarray(a) for a in
                 (y[:SEQ].reshape(1, SEQ, D), y[SEQ:].reshape(SB, ST, D), kp, vp, cp, mk, mv, ks, vs, cs))
```
